# Optimizing a Trainium2 kernel written in Bass

```python
import math
import jax, jax.numpy as jnp
from jax import lax
import numpy as np

D_MODEL = 2048
BATCH = 1
SEQ = 256
DEPTH = 1
DEC_BATCH = 8
DEC_SEQ = 4
PAST_LEN = 2048
PAGE_SIZE = 128

N_MIXERS = 4
D_MIX = D_MODEL
D_GROUP = D_MIX // N_MIXERS
N_SUB = 4
D_SUB = D_GROUP // N_SUB
N_PROJ = 8
CONV_A_W = 31
POOL_WINDOWS = (2, 4, 8, 16)
POOL_BUF = max(POOL_WINDOWS) - 1
SCONV_W = 3
CHUNK = 128
D_FF = int(math.ceil(D_MODEL * 8 / 3 / 256) * 256)
EPS = 1e-6

kernel_name = "hybrid_conv_pool_sconv_sgu_decoder_step"

def rmsnorm(x, g):
    xf = x.astype(jnp.float32)
    y = xf * lax.rsqrt(jnp.mean(xf * xf, axis=-1, keepdims=True) + EPS)
    return (y * g.astype(jnp.float32)).astype(x.dtype)

def layernorm(x, g, b):
    xf = x.astype(jnp.float32)
    mu = jnp.mean(xf, axis=-1, keepdims=True)
    var = jnp.mean(jnp.square(xf - mu), axis=-1, keepdims=True)
    y = (xf - mu) * lax.rsqrt(var + EPS)
    return (y * g.astype(jnp.float32) + b.astype(jnp.float32)).astype(x.dtype)

def causal_dwconv(buf, z, w):
    width, c = w.shape
    zp = jnp.concatenate([buf.astype(z.dtype), z], axis=1)
    y = lax.conv_general_dilated(zp, w[:, None, :].astype(z.dtype), window_strides=(1,), padding='VALID',
                                 dimension_numbers=('NWC', 'WIO', 'NWC'), feature_group_count=c)
    return y, zp[:, -(width - 1):]

def causal_multiscale_pool(buf, p, pos):
    b, l, c = p.shape
    pp = jnp.concatenate([buf.astype(p.dtype), p], axis=1)
    cs = jnp.cumsum(pp.astype(jnp.float32), axis=1)
    cs = jnp.concatenate([jnp.zeros((b, 1, c), jnp.float32), cs], axis=1)
    off = POOL_BUF + 1
    means = []
    for gi, w in enumerate(POOL_WINDOWS):
        sl = slice(gi * D_SUB, (gi + 1) * D_SUB)
        s = cs[:, off:off + l, sl] - cs[:, off - w:off - w + l, sl]
        cnt = jnp.minimum(pos + 1, w).astype(jnp.float32)[None, :, None]
        means.append(s / cnt)
    mean = jnp.concatenate(means, axis=-1)
    return (mean - p.astype(jnp.float32)).astype(p.dtype), pp[:, -POOL_BUF:]

def chunk_spatial_mix(v, w_s, b_s):
    b, l, c = v.shape
    pad = (-l) % CHUNK
    vp = jnp.pad(v, ((0, 0), (0, pad), (0, 0)))
    n = (l + pad) // CHUNK
    vr = vp.reshape(b, n, CHUNK, N_SUB, D_SUB)
    mask = jnp.tril(jnp.ones((CHUNK, CHUNK), v.dtype))
    z = jnp.einsum('gij,bnjgc->bnigc', w_s * mask[None], vr)
    z = z + jnp.transpose(b_s)[None, None, :, :, None]
    return z.reshape(b, n * CHUNK, c)[:, :l]

def mixing_sublayer(x, buf_a, buf_p, buf_c, pos, norm_mix_g, w_in, conv_a_w, conv_a_b, ln_a_g, ln_a_b,
                    pool_w, pool_scale, sconv_w, sgu_ln_g, sgu_ln_b, sgu_w, sgu_b, out_norm_g, w_out):
    b, l, _ = x.shape
    xn = rmsnorm(x, norm_mix_g)
    proj = jnp.einsum('bld,de->ble', xn, w_in)
    a_val, a_gate, p, c_h, c_b, c_c, d_u, d_v = jnp.split(proj, N_PROJ, axis=-1)
    glu = a_val * jax.nn.sigmoid(a_gate)
    ya, nbuf_a = causal_dwconv(buf_a, glu, conv_a_w)
    ya = jax.nn.silu(layernorm(ya + conv_a_b, ln_a_g, ln_a_b))
    pooled, nbuf_p = causal_multiscale_pool(buf_p, p, pos)
    yb = jnp.einsum('blgc,gcd->blgd', pooled.reshape(b, l, N_SUB, D_SUB), pool_w).reshape(b, l, D_GROUP)
    yb = yb * pool_scale
    yc_conv, nbuf_c = causal_dwconv(buf_c, c_c * c_h, sconv_w)
    yc = c_b * yc_conv
    vn = layernorm(d_v, sgu_ln_g, sgu_ln_b)
    yd = d_u * chunk_spatial_mix(vn, sgu_w, sgu_b)
    mix = jnp.stack([ya, yb, yc, yd], axis=2)
    mix = rmsnorm(mix, out_norm_g.reshape(N_MIXERS, D_GROUP)).reshape(b, l, D_MIX)
    x = x + jnp.einsum('ble,ed->bld', mix, w_out)
    return x, nbuf_a, nbuf_p, nbuf_c, vn

def ffn_sublayer(x, norm_ffn_g, w_gate, w_up, w_down):
    xn = rmsnorm(x, norm_ffn_g)
    h = jax.nn.silu(jnp.einsum('bld,df->blf', xn, w_gate)) * jnp.einsum('bld,df->blf', xn, w_up)
    return x + jnp.einsum('blf,fd->bld', h, w_down)

def setup_inputs(seed: int = 0) -> dict:
    key = jax.random.key(seed)
    ks = jax.random.split(key, 32)
    f32 = jnp.float32
    nrm = lambda k, shape, s: jax.random.normal(k, shape, f32) * s
    return {
        "x_prompt": nrm(ks[0], (BATCH, SEQ, D_MODEL), 1.0),
        "x_sample": nrm(ks[1], (DEC_BATCH, DEC_SEQ, D_MODEL), 1.0),
        "state_conv_a": nrm(ks[2], (DEPTH, DEC_BATCH, CONV_A_W - 1, D_GROUP), 0.5),
        "state_pool": nrm(ks[3], (DEPTH, DEC_BATCH, POOL_BUF, D_GROUP), 1.0),
        "state_sconv": nrm(ks[4], (DEPTH, DEC_BATCH, SCONV_W - 1, D_GROUP), 0.5),
        "norm_mix_g": 1.0 + nrm(ks[5], (DEPTH, D_MODEL), 0.05),
        "w_in": nrm(ks[6], (DEPTH, D_MODEL, N_PROJ * D_GROUP), D_MODEL ** -0.5),
        "conv_a_w": nrm(ks[7], (DEPTH, CONV_A_W, D_GROUP), CONV_A_W ** -0.5),
        "conv_a_b": nrm(ks[8], (DEPTH, D_GROUP), 0.02),
        "ln_a_g": 1.0 + nrm(ks[9], (DEPTH, D_GROUP), 0.05),
        "ln_a_b": nrm(ks[10], (DEPTH, D_GROUP), 0.02),
        "pool_w": nrm(ks[11], (DEPTH, N_SUB, D_SUB, D_SUB), D_SUB ** -0.5),
        "pool_scale": 1.0 + nrm(ks[12], (DEPTH, D_GROUP), 0.1),
        "sconv_w": nrm(ks[13], (DEPTH, SCONV_W, D_GROUP), SCONV_W ** -0.5),
        "sgu_ln_g": 1.0 + nrm(ks[14], (DEPTH, D_GROUP), 0.05),
        "sgu_ln_b": nrm(ks[15], (DEPTH, D_GROUP), 0.02),
        "sgu_w": nrm(ks[16], (DEPTH, N_SUB, CHUNK, CHUNK), CHUNK ** -0.5),
        "sgu_b": 1.0 + nrm(ks[17], (DEPTH, N_SUB, CHUNK), 0.05),
        "out_norm_g": 1.0 + nrm(ks[18], (DEPTH, D_MIX), 0.05),
        "w_out": nrm(ks[19], (DEPTH, D_MIX, D_MODEL), D_MIX ** -0.5),
        "norm_ffn_g": 1.0 + nrm(ks[20], (DEPTH, D_MODEL), 0.05),
        "w_gate": nrm(ks[21], (DEPTH, D_MODEL, D_FF), D_MODEL ** -0.5),
        "w_up": nrm(ks[22], (DEPTH, D_MODEL, D_FF), D_MODEL ** -0.5),
        "w_down": nrm(ks[23], (DEPTH, D_FF, D_MODEL), D_FF ** -0.5),
        "final_norm_g": 1.0 + nrm(ks[24], (D_MODEL,), 0.05),
    }

def reference(x_prompt, x_sample, state_conv_a, state_pool, state_sconv, norm_mix_g, w_in, conv_a_w,
              conv_a_b, ln_a_g, ln_a_b, pool_w, pool_scale, sconv_w, sgu_ln_g, sgu_ln_b, sgu_w, sgu_b,
              out_norm_g, w_out, norm_ffn_g, w_gate, w_up, w_down, final_norm_g):
    b_p, l_p, _ = x_prompt.shape
    pos_p = jnp.arange(l_p, dtype=jnp.int32)
    pos_s = PAST_LEN + jnp.arange(x_sample.shape[1], dtype=jnp.int32)
    dt = x_prompt.dtype
    zero_a = jnp.zeros((b_p, CONV_A_W - 1, D_GROUP), dt)
    zero_p = jnp.zeros((b_p, POOL_BUF, D_GROUP), dt)
    zero_c = jnp.zeros((b_p, SCONV_W - 1, D_GROUP), dt)
    hp, hs = x_prompt, x_sample
    ca_p, ca_s, pl_p, pl_s, sc_p, sc_s, v_s = [], [], [], [], [], [], []
    for l in range(DEPTH):
        params = (norm_mix_g[l], w_in[l], conv_a_w[l], conv_a_b[l], ln_a_g[l], ln_a_b[l], pool_w[l],
                  pool_scale[l], sconv_w[l], sgu_ln_g[l], sgu_ln_b[l], sgu_w[l], sgu_b[l], out_norm_g[l],
                  w_out[l])
        hp, na, npl, nc, _ = mixing_sublayer(hp, zero_a, zero_p, zero_c, pos_p, *params)
        ca_p.append(na); pl_p.append(npl); sc_p.append(nc)
        hs, na, npl, nc, vn = mixing_sublayer(hs, state_conv_a[l], state_pool[l], state_sconv[l], pos_s, *params)
        ca_s.append(na); pl_s.append(npl); sc_s.append(nc); v_s.append(vn)
        hp = ffn_sublayer(hp, norm_ffn_g[l], w_gate[l], w_up[l], w_down[l])
        hs = ffn_sublayer(hs, norm_ffn_g[l], w_gate[l], w_up[l], w_down[l])
    y_prompt = rmsnorm(hp, final_norm_g)
    y_sample = rmsnorm(hs, final_norm_g)
    return (y_prompt, y_sample, jnp.stack(ca_p), jnp.stack(ca_s), jnp.stack(pl_p), jnp.stack(pl_s),
            jnp.stack(sc_p), jnp.stack(sc_s), jnp.stack(v_s))


_drawn_inputs = setup_inputs


def setup_inputs(seed=0):
    import zlib

    import numpy as np

    out = dict(_drawn_inputs(seed))
    spreads = {}
    factors = {'conv_a_b': 3.422, 'ln_a_b': 7.105, 'sgu_ln_b': 2.856, 'sgu_b': 4.098}
    for name, (base, spread) in spreads.items():
        noise = np.random.default_rng([zlib.crc32(name.encode()), seed]).standard_normal(out[name].shape)
        drawn = base * np.exp(spread * noise) if base else spread * noise
        out[name] = __import__('jax').numpy.asarray(drawn.astype(out[name].dtype))
    for name, factor in factors.items():
        out[name] = (out[name] * factor).astype(out[name].dtype)
    return out
```

```python
from contextlib import ExitStack

import concourse.bass as bass
from concourse import mybir
from concourse.alu_op_type import AluOpType as ALU

ACT = mybir.ActivationFunctionType
F32 = mybir.dt.float32
F32R = mybir.dt.float32r

P = 128
D = 2048
KD = D // P
SEQ = 256
NB, NS = 8, 4
T = SEQ + NB * NS
GRP = 512
NG = GRP // P
F = 5632
NF = F // GRP
CW = 31
PW = 15
SW = 3
EPS = 1e-6

TK = 2
TILE = TK * GRP
RING = 4
BANKS = 6
AHEAD = RING - 1

GA, GS = CW - 1 + SEQ, CW - 1 + NS
PA, PS = PW + SEQ, PW + NS
CA, CS = SW - 1 + SEQ, SW - 1 + NS
GL, PL, CL = GA + NB * GS, PA + NB * PS, CA + NB * CS

A_VAL, A_GATE, POOL, C_H, C_B, C_C, D_U, D_V = range(8)
STRIPS = [A_GATE, A_VAL, POOL, D_V, D_U, C_H, C_C, C_B]
MIX_A, MIX_B, MIX_C, MIX_D = range(4)
OUT_ORDER = [MIX_B, MIX_D, MIX_C, MIX_A]

PER = D // (TK * P)
T_IN = 0
T_OUT = T_IN + len(STRIPS) * PER
T_G0 = T_OUT + (D // GRP) * PER
T_U0 = T_G0 + PER
T_LOOP = T_U0 + PER
PER_DN = GRP // (TK * P)
BODY = 2 * PER + (D // GRP) * PER_DN
T_END = T_LOOP + (NF - 1) * BODY
TILES = T_END + (D // GRP) * PER_DN

S_OUT = len(STRIPS)
S_G0 = S_OUT + D // GRP
S_U0 = S_G0 + 1
S_LOOP = S_U0 + 1
S_BODY = 2 + D // GRP
S_END = S_LOOP + (NF - 1) * S_BODY
S_ALL = S_END + D // GRP
assert S_BODY * NG % BANKS == 0 and BODY % RING == 0

VECS = [("norm_mix_g", KD), ("conv_a_b", NG), ("ln_a_g", NG), ("ln_a_b", NG), ("pool_scale", NG),
        ("sgu_ln_g", NG), ("sgu_ln_b", NG), ("out_norm_g", KD), ("norm_ffn_g", KD), ("final_norm_g", KD),
        ("sconv_w", SW * NG)]
VROW, NV = {}, 0
for _name, _rows in VECS:
    VROW[_name] = NV
    NV += _rows

NORM = {n: i for i, n in enumerate(["s1", "b_rms", "d_var", "d_rms", "a_var", "c_rms", "a_rms", "s2", "s3"])}
_BY_ACT = ["vecs", "sgu_w", "st_a0", "st_a1", "st_a2", "st_a3", "st_p", "st_c", "new_ap", "new_as", "new_pp",
           "new_ps", "b0", "b1", "b2", "b3", "vt0", "vt1", "vt2", "new_cp", "new_cs"]
ACT_COUNT = {n: i + 1 for i, n in enumerate(_BY_ACT)}
TAKEN = {n: ("misc_act", ACT_COUNT[n]) for n in _BY_ACT}
TAKEN.update({n: ("var_ready", i + 1) for n, i in NORM.items()})
TAKEN.update({"d_mean": ("d_cent", NG), "a_mean": ("a_cent", NG)})
TAKEN.update({f"z{n}": ("d_out", n + 1) for n in range(NG)})
MISC = ["vecs", "sgu_w", "s1", "st_a0", "st_a1", "st_a2", "st_a3", "st_p", "st_c", "new_ap", "new_as", "new_pp",
        "new_ps", "b0", "b1", "b2", "b3", "b_rms", "d_mean", "d_var", "vt0", "vt1", "vt2", "z0", "z1", "z2", "z3",
        "d_rms", "new_cp", "new_cs", "a_mean", "a_var", "c_rms", "a_rms", "s2", "s3"]
MISC_AT = {name: i for i, name in enumerate(MISC)}

TAPS = {16: 2, 17: 2, 18: 2, 19: 2, 20: 2, 21: 2, 22: 2, 29: 1, 30: 1, 38: 1, 43: 2, 44: 2, 45: 1, 46: 1,
        50: 1, 51: 1, 52: 1, 53: 1, 54: 1, 56: 1, 57: 1, 58: 1}
assert sum(TAPS.values()) == CW


def full_at(strip, n):
    return KD + (NG - 1) * strip + n + 1


def use_of(strip, n):
    return KD + NG * strip + n


def hybrid_step(nc, a, o):
    ctx = ExitStack()
    with ctx:
        def sb(name, cols, dt=F32):
            return ctx.enter_context(nc.sbuf_tensor(name, [P, cols], dt))

        def sem(name):
            return ctx.enter_context(nc.semaphore(name))

        def blocks(t, n=NG):
            return t.rearrange("p (n t) -> p n t", n=n)

        x_sb = sb("x_sb", KD * T)
        xh_sb, xl_sb = sb("xh_sb", KD * T, F32R), sb("xl_sb", KD * T, F32R)
        mh_sb, ml_sb = sb("mh_sb", KD * T, F32R), sb("ml_sb", KD * T, F32R)
        raw = sb("raw", RING * TILE)
        wh, wl = sb("wh", RING * TILE, F32R), sb("wl", RING * TILE, F32R)
        X = blocks(x_sb[:, :], KD)
        XH, XL = blocks(xh_sb[:, :], KD), blocks(xl_sb[:, :], KD)
        MH, ML = blocks(mh_sb[:, :], KD), blocks(ml_sb[:, :], KD)

        work = sb("work", 3 * D)
        stage = work[:, :].rearrange("p (c d) -> p c d", c=3)
        NT = NG * T
        T0, T1, T2 = (blocks(work[:, i * NT:(i + 1) * NT]) for i in range(3))
        vt = work[:, 3 * NT:3 * NT + 3 * GRP].rearrange("p (c d) -> p c d", c=3)
        T4 = blocks(work[:, 3 * NT + 3 * GRP:4 * NT + 3 * GRP])
        st_a = work[:, NT:NT + 2 * GRP].rearrange("p (h d) -> p h d", h=2)
        st_p = work[:, NT + 2 * GRP:NT + 3 * GRP]
        st_c = work[:, NT + 3 * GRP:NT + 4 * GRP]
        sgu_rows = work[:, NT + 4 * GRP:NT + 5 * GRP]
        new_p = work[:, 4 * NT:4 * NT + 2 * GRP].rearrange("p (c d) -> p c d", c=2)

        g_sb, p_sb, c_sb = sb("g_sb", NG * GL), sb("p_sb", NG * PL), sb("c_sb", NG * CL)
        G, PP, C = blocks(g_sb[:, :]), blocks(p_sb[:, :]), blocks(c_sb[:, :])
        SG = blocks(g_sb[:, 0:NT])
        HU = blocks(p_sb[:, 0:NT])
        sq_sb = sb("sq_sb", NT)
        SQ = blocks(sq_sb[:, :])
        vec_rows, tap_rows = sq_sb[:, 0:P], sq_sb[:, P:2 * P]
        new_a = sq_sb[:, 0:2 * GRP].rearrange("p (c d) -> p c d", c=2)
        pair = sb("pair", 3 * T)
        S_A, S_B = pair[:, 0:PL], pair[:, PL:2 * PL]
        norm0 = sb("norm0", 3 * T)
        SETS = [[t[:, i * T:(i + 1) * T] for i in range(3)] for t in (norm0, pair)]
        s_bc = sb("s_bc", T)
        sum_sq, one_sq = sb("sum_sq", T), sb("one_sq", T)

        ident, ones, ones_d, ones_g = (sb(n, P) for n in ("ident", "ones", "ones_d", "ones_g"))
        vec, taps = sb("vec", NV), sb("taps", CW * NG)
        wt = sb("wt", NG * P)
        bd = sb("bd", NG * NB * NS)
        pw = sb("pw", NG * P)
        brow = sb("brow", NG * P)
        inv = sb("inv", PW + 1)
        tails = sb("tails", NG * NB * NS)
        WT, BD = blocks(wt[:, :]), blocks(bd[0:NB * NS, :])
        PWV, BROW = blocks(pw[:, :]), blocks(brow[0:1, :])

        def v(name, b):
            return vec[:, VROW[name] + b:VROW[name] + b + 1]

        def tap(k, b):
            return taps[:, k * NG + b:k * NG + b + 1]

        def halves(buf, b, width, first, at, n):
            prompt = buf[:, b, at:at + first]
            sample = buf[:, b, width:].rearrange("p (s r) -> p s r", s=NB)[:, :, at:at + n]
            return prompt, sample

        def g_at(b, k):
            return halves(G, b, GA, SEQ, k, NS)

        def p_at(b, k):
            return halves(PP, b, PA, SEQ, k, NS)

        def c_at(b, k):
            return halves(C, b, CA, SEQ, k, NS)

        def two(t):
            return t[:, 0:SEQ], t[:, SEQ:T].rearrange("p (s r) -> p s r", s=NB)

        bank = [ctx.enter_context(nc.psum_tensor(f"bank{i}", [P, 512], F32)) for i in range(BANKS + 2)]

        raw_landed = [sem(f"raw_landed{i}") for i in range(RING)]
        x_landed = [sem(f"x_landed{i}") for i in range(3)]
        vecs_landed, sgu_landed, late_landed, mats_landed, corner_landed = (sem(n) for n in (
            "vecs_landed", "sgu_landed", "late_landed", "mats_landed", "corner_landed"))
        hi_ready, lo_ready, tile_used = sem("hi_ready"), sem("lo_ready"), sem("tile_used")
        banks_full, banks_free = sem("banks_full"), sem("banks_free")
        misc_full, misc_act = sem("misc_full"), sem("misc_act")
        x_hi, x_lo, y_hi, y_lo = sem("x_hi"), sem("x_lo"), sem("y_hi"), sem("y_lo")
        const_ready, pads_ready, bd_zero, masked = (sem(n) for n in ("const_ready", "pads_ready", "bd_zero", "masked"))
        sums, pool_chain, dve_chain, act_chain = (sem(n) for n in ("sums", "pool_chain", "dve_chain", "act_chain"))
        var_ready, sd_ready, r_ready = sem("var_ready"), sem("sd_ready"), sem("r_ready")
        gate_sig, glu_ready, conv_done = sem("gate_sig"), sem("glu_ready"), sem("conv_done")
        pin_ready, cin_ready, pooled = sem("pin_ready"), sem("cin_ready"), sem("pooled")
        d_cent, d_unit, vn_ready, d_out = sem("d_cent"), sem("d_unit"), sem("vn_ready"), sem("d_out")
        a_cent, a_unit, a_act, a_out = sem("a_cent"), sem("a_unit"), sem("a_act"), sem("a_out")
        squares = sem("squares")
        scaled = [sem(f"scaled{m}") for m in range(4)]
        mix_hi, mix_lo = [sem(f"mix_hi{m}") for m in range(4)], [sem(f"mix_lo{m}") for m in range(4)]
        tails_ready, ffn_silu, ffn_scaled = sem("tails_ready"), sem("ffn_silu"), sem("ffn_scaled")
        ffn_sig, h_hi, h_lo = sem("ffn_sig"), sem("h_hi"), sem("h_lo")
        a_stored, b_stored, v_stored, c_stored, kept = (sem(n) for n in (
            "a_stored", "b_stored", "v_stored", "c_stored", "kept"))
        out_scaled, out_dve, out_act, y_stored = (sem(n) for n in ("out_scaled", "out_dve", "out_act", "y_stored"))
        SEMS = {"misc_act": misc_act, "var_ready": var_ready, "d_cent": d_cent, "a_cent": a_cent, "d_out": d_out}

        def w_rows(w, row, col):
            return w[row:row + TK * P, col:col + GRP].rearrange("(k p) n -> p k n", k=TK)

        def tile_source(t):
            if t < T_OUT:
                s, kt = divmod(t, PER)
                return w_rows(a["w_in"], kt * TK * P, STRIPS[s] * GRP)
            if t < T_G0:
                s, kt = divmod(t - T_OUT, PER)
                m, half = OUT_ORDER[kt // 2], kt % 2
                return w_rows(a["w_out"], m * GRP + half * TK * P, s * GRP)
            if t < T_U0:
                return w_rows(a["w_gate"], (t - T_G0) * TK * P, 0)
            if t < T_LOOP:
                return w_rows(a["w_up"], (t - T_U0) * TK * P, 0)
            s, kt = divmod(t - T_END, PER_DN)
            return w_rows(a["w_down"], (NF - 1) * GRP + kt * TK * P, s * GRP)

        def loop_source(g, j):
            if j < PER or j >= BODY - PER:
                w, kt = (a["w_gate"], j) if j < PER else (a["w_up"], j - (BODY - PER))
                return w[kt * TK * P:(kt + 1) * TK * P, bass.ds(g * GRP + GRP, GRP)].rearrange("(k p) n -> p k n", k=TK)
            s, kt = divmod(j - PER, PER_DN)
            return w_down_rows(g, kt)[:, :, s * GRP:(s + 1) * GRP]

        def w_down_rows(g, kt):
            return a["w_down"][bass.ds(g * GRP + kt * TK * P, TK * P), :].rearrange("(k p) n -> p k n", k=TK)

        def slot(buf, t):
            return buf[:, (t % RING) * TILE:(t % RING + 1) * TILE]

        class Chain:
            def __init__(self, eng, s):
                self.eng, self.s, self.n = eng, s, 0

            def __call__(self, ins):
                self.n += 1
                ins.then_inc(self.s, 1)
                self.eng.wait_ge(self.s, self.n)

        def misc_bank(name):
            return bank[BANKS + MISC_AT[name] % 2]

        block = ctx.enter_context(nc.Block())

        Y_PARTS = [(P, 0, 2), (NB * NS, 2, 3)]

        def y_rows(c, q):
            if c < 2:
                return raw[:, c * D + q * GRP:c * D + (q + 1) * GRP]
            return work[:, 3 * NT + q * GRP:3 * NT + (q + 1) * GRP]

        @block.sync
        def _(sp):
            xp = a["x_prompt"][0]
            xs = a["x_sample"].rearrange("b t d -> (b t) d")
            for c in range(2):
                sp.dma_start(stage[:, c, :], xp[c * P:(c + 1) * P, :]).then_inc(x_landed[c], 16)
            sp.dma_start(stage[0:NB * NS, 2, :], xs).then_inc(x_landed[2], 16)

            def load(t, src, lo_count, landed_in):
                if lo_count is not None:
                    sp.wait_ge(lo_ready, lo_count)
                sp.dma_start(slot(raw, t).rearrange("p (k n) -> p k n", k=TK), src).then_inc(raw_landed[landed_in], 16)

            for t in range(T_LOOP):
                load(t, tile_source(t), t - RING + 1 if t >= RING else None, t % RING)
            with sp.Fori(0, NF - 1) as g:
                for j in range(BODY):
                    t = T_LOOP + j
                    load(t, loop_source(g, j), g * BODY + (t - RING + 1), t % RING)
            for t in range(T_END, TILES):
                load(t, tile_source(t), t - RING + 1, t % RING)

            yp, ys = o[0][0], o[1].rearrange("b t d -> (b t) d")
            for w in range(3 * NG):
                c, q = divmod(w, NG)
                sp.wait_ge(out_dve if w % 2 == 0 else out_act, w // 2 + 1)
                n = P if c < 2 else NB * NS
                dst = (yp[c * P:(c + 1) * P, :] if c < 2 else ys)[:, q * GRP:(q + 1) * GRP]
                sp.dma_start(dst, y_rows(c, q)[0:n, :]).then_inc(y_stored, 16)
            sp.wait_ge(y_stored, 16 * 3 * NG)
            sp.wait_ge(kept, 32)
            sp.wait_ge(a_stored, 32)
            sp.wait_ge(b_stored, 32)
            sp.wait_ge(v_stored, 16)
            sp.wait_ge(c_stored, 32)

        @block.gpsimd
        def _(pool):
            chain = Chain(pool, pool_chain)
            chain(pool.memset(ident[:, :], 0.0))
            pool.affine_select(out=ident[:, :], in_=ident[:, :], compare_op=ALU.not_equal, fill=1.0, base=0,
                               pattern=[[-1, P]], channel_multiplier=1).then_inc(const_ready, 1)
            pool.memset(ones[:, :], 1.0).then_inc(const_ready, 1)
            pool.memset(ones_d[:, :], 1.0 / D).then_inc(const_ready, 1)
            pool.memset(ones_g[:, :], 1.0 / GRP).then_inc(const_ready, 1)
            pool.memset(bd[0:NB * NS, :], 0.0).then_inc(bd_zero, 1)
            pool.memset(G[:, :, 0:CW - 1], 0.0).then_inc(pads_ready, 1)
            pool.memset(PP[:, :, 0:PW], 0.0).then_inc(pads_ready, 1)
            pool.memset(C[:, :, 0:SW - 1], 0.0).then_inc(pads_ready, 1)
            for t in range(PW):
                last = pool.memset(inv[:, t:t + 1], 1.0 / (t + 1))
            last.then_inc(pads_ready, 1)

            def sum_squares(b, ready, count):
                pool.wait_ge(ready, count)
                if b == 0:
                    chain(pool.tensor_tensor(sum_sq[:, :], X[:, b, :], X[:, b, :], ALU.mult))
                    return
                chain(pool.tensor_tensor(one_sq[:, :], X[:, b, :], X[:, b, :], ALU.mult))
                ins = pool.tensor_tensor(sum_sq[:, :], sum_sq[:, :], one_sq[:, :], ALU.add)
                if b == KD - 1:
                    ins.then_inc(sums, 1)
                else:
                    chain(ins)

            for b in range(KD):
                sum_squares(b, banks_free, b + 1)

            pool.wait_ge(misc_act, ACT_COUNT["sgu_w"])
            pool.affine_select(out=WT, in_=WT, compare_op=ALU.is_ge, fill=0.0, base=0,
                               pattern=[[0, NG], [1, P]], channel_multiplier=-1).then_inc(masked, 1)

            pool.wait_ge(misc_full, MISC_AT["s1"] + 1)
            for b in range(KD):
                sum_squares(b, banks_free, use_of(S_OUT + b // NG, b % NG) + 1)
            pool.wait_ge(misc_full, MISC_AT["s2"] + 1)
            for b in range(KD):
                sum_squares(b, banks_free, use_of(S_END + b // NG, b % NG) + 1)

        @block.scalar
        def _(act):
            chain = Chain(act, act_chain)
            for name, rows in VECS:
                src = a[name].rearrange("(r p) -> r p", p=P)
                act.dma_start(vec_rows[VROW[name]:VROW[name] + rows, :], src).then_inc(vecs_landed, 16)
            act.dma_start(tap_rows[0:CW * NG, :], a["conv_a_w"].rearrange("k (b p) -> (k b) p", p=P)).then_inc(vecs_landed, 16)
            act.dma_start(PWV, a["pool_w"].rearrange("g c d -> c g d")).then_inc(mats_landed, 16)
            act.dma_start(brow[0:1, :], a["sgu_b"].rearrange("(u g) i -> u (g i)", u=1)).then_inc(mats_landed, 16)
            act.dma_start(o[3][0, :, 0:CW - 1 - NS, :], a["state_conv_a"][:, NS:, :]).then_inc(kept, 16)
            act.dma_start(o[5][0, :, 0:PW - NS, :], a["state_pool"][:, NS:, :]).then_inc(kept, 16)

            def copy_out(name, *pairs):
                act.wait_ge(misc_full, MISC_AT[name] + 1)
                for dst, src in pairs[:-1]:
                    act.activation(dst, src, ACT.Copy)
                act.activation(*pairs[-1], ACT.Copy).then_inc(misc_act, 1)

            def hi(t, landed, used):
                act.wait_ge(raw_landed[t % RING], landed)
                if used is not None:
                    act.wait_ge(tile_used, used)
                act.activation(slot(wh, t), slot(raw, t), ACT.Copy).then_inc(hi_ready, 1)

            def hi_at(t):
                if t < TILES:
                    hi(t, 16 * (t // RING + 1), t - RING + 1 if t >= RING else None)

            def square(src, ready, count, prior=None):
                act.wait_ge(ready, count)
                if prior is not None:
                    act.wait_ge(misc_full, MISC_AT[prior] + 1)
                for b in range(NG):
                    act.activation(SQ[:, b, :], src[:, b, :], ACT.Square).then_inc(squares, 1)

            def root(k):
                act.wait_ge(var_ready, k + 1)
                s = SETS[1 if k == NORM["a_rms"] or k == NORM["a_var"] else 0]
                act.activation(s[1], s[0], ACT.Sqrt).then_inc(sd_ready, 1)

            def mixer_hi(m, src):
                for b in range(NG):
                    act.wait_ge(scaled[m], b + 1)
                    act.activation(MH[:, m * NG + b, :], src[:, b, :], ACT.Copy).then_inc(mix_hi[m], 1)

            def dense_tails(buf, width, at, n, count):
                act.wait_ge(banks_free, count)
                src = buf[:, :, width:].rearrange("p b (s r) -> p b s r", s=NB)[:, :, :, at:at + n]
                dst = tails[:, 0:NG * NB * n].rearrange("p (b s r) -> p b s r", b=NG, s=NB)
                act.activation(dst, src, ACT.Copy).then_inc(tails_ready, 1)

            M = misc_bank("vecs")
            copy_out("vecs", (vec[:, :], M[:, 0:NV]), (taps[:, :], M[:, P:P + CW * NG]))
            act.wait_ge(misc_act, 1)
            for b in range(KD):
                act.wait_ge(banks_free, b + 1)
                act.activation(XH[:, b, :], X[:, b, :], ACT.Copy, scale=v("norm_mix_g", b)).then_inc(x_hi, 1)
                if b in (3, 5, 7):
                    hi_at((b - 3) // 2)
            act.wait_ge(banks_full, KD)
            act.dma_start(sgu_rows.rearrange("p (g j) -> p g j", g=NG), a["sgu_w"].rearrange("g i j -> i g j")).then_inc(sgu_landed, 16)
            HB = NB // 2
            act.dma_start(st_a[0:HB * (CW - 1), :, :],
                          a["state_conv_a"].rearrange("(h s) t c -> (s t) h c", h=2)).then_inc(late_landed, 16)
            act.dma_start(st_p[0:NB * PW, :], a["state_pool"].rearrange("s t c -> (s t) c")).then_inc(late_landed, 16)
            act.dma_start(st_c[0:NB * (SW - 1), :], a["state_sconv"].rearrange("s t c -> (s t) c")).then_inc(late_landed, 16)

            for t in range(T_LOOP):
                hi_at(t + AHEAD)
                if t == 2:
                    copy_out("sgu_w", (wt[:, :], misc_bank("sgu_w")[:, :]))
                if t == 7:
                    root(NORM["s1"])
                if t == 8:
                    for b in range(NG):
                        act.wait_ge(banks_free, use_of(0, b) + 1)
                        act.activation(T0[:, b, :], T0[:, b, :], ACT.Sigmoid).then_inc(gate_sig, 1)
                if 9 <= t <= 10:
                    for b in (0, 1) if t == 9 else (2, 3):
                        copy_out(f"st_a{b}", (G[:, b, GA:].rearrange("p (s r) -> p s r", s=NB)[:, :, 0:CW - 1],
                                              misc_bank(f"st_a{b}")[:, 0:NB * (CW - 1)].rearrange("p (s r) -> p s r", s=NB)))
                if t == 11:
                    copy_out("st_p", *[(PP[:, b, PA:].rearrange("p (s r) -> p s r", s=NB)[:, :, 0:PW],
                                        misc_bank("st_p")[:, b * P:b * P + NB * PW].rearrange("p (s r) -> p s r", s=NB))
                                       for b in range(NG)])
                    copy_out("st_c", *[(C[:, b, CA:].rearrange("p (s r) -> p s r", s=NB)[:, :, 0:SW - 1],
                                        misc_bank("st_c")[:, b * P:b * P + NB * (SW - 1)].rearrange("p (s r) -> p s r", s=NB))
                                       for b in range(NG)])
                if t == 12:
                    act.wait_ge(masked, 1)
                    act.wait_ge(bd_zero, 1)
                    for s in range(NB):
                        act.dma_start(BD[s * NS:(s + 1) * NS, :, s * NS:(s + 1) * NS],
                                      WT[0:NS, :, 0:NS]).then_inc(corner_landed, 16)
                if t == 16:
                    dense_tails(G, GA, CW - 1, NS, use_of(1, NG - 1) + 1)
                if t == 24:
                    dense_tails(PP, PA, PW, NS, use_of(2, NG - 1) + 1)
                if t == 56:
                    dense_tails(C, CA, NS, SW - 1, use_of(6, NG - 1) + 1)
                if t == 18:
                    copy_out("new_ap", (new_a[0:CW - 1, 0, :], misc_bank("new_ap")[0:CW - 1, :]))
                    copy_out("new_as", (new_a[0:NB * NS, 1, :], misc_bank("new_as")[0:NB * NS, :]))
                    act.wait_ge(misc_act, ACT_COUNT["new_as"])
                    act.dma_start(o[2][0, 0], new_a[0:CW - 1, 0, :]).then_inc(a_stored, 16)
                    act.dma_start(o[3][0, :, CW - 1 - NS:, :], new_a[0:NB * NS, 1, :]).then_inc(a_stored, 16)
                if t == 25:
                    copy_out("new_pp", (new_p[0:PW, 0, :], misc_bank("new_pp")[0:PW, :]))
                    copy_out("new_ps", (new_p[0:NB * NS, 1, :], misc_bank("new_ps")[0:NB * NS, :]))
                    act.wait_ge(misc_act, ACT_COUNT["new_ps"])
                    act.dma_start(o[4][0, 0], new_p[0:PW, 0, :]).then_inc(b_stored, 16)
                    act.dma_start(o[5][0, :, PW - NS:, :], new_p[0:NB * NS, 1, :]).then_inc(b_stored, 16)
                if 27 <= t <= 28:
                    for b in (0, 1) if t == 27 else (2, 3):
                        act.wait_ge(misc_full, MISC_AT[f"b{b}"] + 1)
                        act.activation(T2[:, b, :], misc_bank(f"b{b}")[:, 0:T], ACT.Copy,
                                       scale=v("pool_scale", b)).then_inc(misc_act, 1)
                if t == 28:
                    act.wait_ge(a_stored, 32)
                    square(T2, misc_act, ACT_COUNT["b3"])
                if t == 29:
                    root(NORM["b_rms"])
                if t == 31:
                    mixer_hi(MIX_B, T2)
                if t == 34:
                    square(T0, d_cent, NG, "b_rms")
                if t == 35:
                    root(NORM["d_var"])
                if t == 37:
                    for b in range(NG):
                        act.wait_ge(d_unit, b + 1)
                        act.activation(T0[:, b, :], T0[:, b, :], ACT.Identity, bias=v("sgu_ln_b", b),
                                       scale=v("sgu_ln_g", b)).then_inc(vn_ready, 1)
                if t == 38:
                    act.wait_ge(b_stored, 32)
                    copy_out("vt0", (vt[:, 0, :], misc_bank("vt0")[:, :]))
                    copy_out("vt1", (vt[:, 1, :], misc_bank("vt1")[:, :]))
                if t == 39:
                    copy_out("vt2", (vt[0:NB * NS, 2, :], misc_bank("vt2")[0:NB * NS, :]))
                    act.wait_ge(misc_act, ACT_COUNT["vt2"])
                    act.dma_start(o[8][0].rearrange("b t c -> (b t) c"), vt[0:NB * NS, 2, :]).then_inc(v_stored, 16)
                if t == 42:
                    square(T4, d_out, NG, "d_var")
                if t == 43:
                    root(NORM["d_rms"])
                if t == 45:
                    mixer_hi(MIX_D, T4)
                if t == 57:
                    act.wait_ge(v_stored, 16)
                    copy_out("new_cp", (vt[0:SW - 1, 0, :], misc_bank("new_cp")[0:SW - 1, :]))
                    copy_out("new_cs", (vt[0:NB * (SW - 1), 1, :], misc_bank("new_cs")[0:NB * (SW - 1), :]))
                    act.wait_ge(misc_act, ACT_COUNT["new_cs"])
                    act.dma_start(o[6][0, 0], vt[0:SW - 1, 0, :]).then_inc(c_stored, 16)
                    act.dma_start(o[7][0].rearrange("b t c -> (b t) c"), vt[0:NB * (SW - 1), 1, :]).then_inc(c_stored, 16)
                if t == 60:
                    square(T1, a_cent, NG, "d_rms")
                if t == 61:
                    root(NORM["a_var"])
                if t == 63:
                    for b in range(NG):
                        act.wait_ge(a_unit, b + 1)
                        act.activation(SG[:, b, :], T1[:, b, :], ACT.Sigmoid, bias=v("ln_a_b", b),
                                       scale=v("ln_a_g", b))
                        act.activation(T1[:, b, :], T1[:, b, :], ACT.Identity, bias=v("ln_a_b", b),
                                       scale=v("ln_a_g", b)).then_inc(a_act, 1)
                if t == 64:
                    square(T2, banks_free, use_of(S_OUT - 1, NG - 1) + 1, "a_var")
                if t == 65:
                    root(NORM["c_rms"])
                    square(T1, a_out, NG, "c_rms")
                if t == 66:
                    root(NORM["a_rms"])
                if t == 67:
                    mixer_hi(MIX_C, T2)
                if t == 68:
                    mixer_hi(MIX_A, T1)
                if T_OUT < t <= T_G0 and t % PER == 0:
                    for b in range((t - T_OUT) // PER * NG - NG, (t - T_OUT) // PER * NG):
                        act.wait_ge(banks_free, use_of(S_OUT + b // NG, b % NG) + 1)
                        act.activation(XH[:, b, :], X[:, b, :], ACT.Copy, scale=v("norm_ffn_g", b)).then_inc(y_hi, 1)
                if t == T_G0 + 4:
                    root(NORM["s2"])
                if t == T_U0:
                    for b in range(NG):
                        act.wait_ge(banks_free, use_of(S_G0, b) + 1)
                        act.activation(T0[:, b, :], SG[:, b, :], ACT.Sigmoid).then_inc(ffn_sig, 1)

            def hidden_hi(count):
                for b in range(NG):
                    act.wait_ge(banks_free, count + b + 1)
                    act.activation(MH[:, b, :], HU[:, b, :], ACT.Copy).then_inc(h_hi, 1)

            with act.Fori(0, NF - 1) as g:
                for j in range(BODY):
                    t = T_LOOP + j + AHEAD
                    hi(t, g * (16 * BODY // RING) + 16 * (t // RING + 1), g * BODY + (t - RING + 1))
                    if j == 0:
                        hidden_hi(g * (S_BODY * NG) + use_of(S_LOOP - 1, 0))
                    if j == PER:
                        for b in range(NG):
                            act.wait_ge(banks_free, g * (S_BODY * NG) + (use_of(S_LOOP, b) + 1))
                            act.activation(T0[:, b, :], SG[:, b, :], ACT.Sigmoid).then_inc(ffn_sig, 1)
            for t in range(T_END, TILES):
                hi_at(t + AHEAD)
                if t == T_END:
                    hidden_hi(use_of(S_END - 1, 0))
            act.wait_ge(sums, 3)
            for b in range(KD):
                act.activation(X[:, b, :], X[:, b, :], ACT.Copy, scale=v("final_norm_g", b)).then_inc(out_scaled, 1)
            act.wait_ge(var_ready, NORM["s3"] + 1)
            for n, c0, c1 in Y_PARTS:
                ins = act.activation(norm0[0:n, 3 + c0:3 + c1], norm0[0:n, c0:c1], ACT.Sqrt)
            ins.then_inc(sd_ready, 1)
            act.wait_ge(r_ready, 1)
            act.wait_ge(c_stored, 32)
            for w in range(1, 3 * NG, 2):
                c, q = divmod(w, NG)
                n = P if c < 2 else NB * NS
                act.wait_ge(banks_full, full_at(S_ALL, 0) + w)
                act.activation(y_rows(c, q)[0:n, :], bank[(use_of(S_ALL, 0) + w) % BANKS][0:n, :], ACT.Copy,
                               scale=norm0[0:n, 9 + c:10 + c]).then_inc(out_act, 1)

        @block.vector
        def _(dve):
            chain = Chain(dve, dve_chain)
            taps_done = [0]

            def lo(t, count):
                dve.wait_ge(hi_ready, count)
                dve.tensor_tensor(slot(wl, t), slot(raw, t), slot(wh, t).bitcast(F32), ALU.subtract).then_inc(lo_ready, 1)

            def lo_at(t):
                if t < TILES:
                    lo(t, t + 1)

            def strip_block(strip, n, last_tile):
                if n < NG - 1:
                    dve.wait_ge(banks_full, full_at(strip, n))
                else:
                    dve.wait_ge(tile_used, last_tile + 1)
                return bank[use_of(strip, n) % BANKS]

            def in_block(strip, n):
                return strip_block(strip, n, (strip + 1) * PER - 1)

            def x_part(b):
                dve.wait_ge(x_hi, b + 1)
                dve.scalar_tensor_tensor(out=XL[:, b, :], in0=X[:, b, :], scalar=v("norm_mix_g", b),
                                         in1=XH[:, b, :].bitcast(F32), op0=ALU.mult, op1=ALU.subtract).then_inc(x_lo, 1)

            def var_out(name, k_set=0):
                dve.wait_ge(misc_full, MISC_AT[name] + 1)
                dve.tensor_scalar(SETS[k_set][0], misc_bank(name)[:, 0:T], EPS, None, ALU.add).then_inc(var_ready, 1)

            def inv_root(k, dst, k_set=0):
                var, r, t = SETS[k_set]
                dve.wait_ge(sd_ready, k + 1)
                chain(dve.reciprocal(r, r))
                chain(dve.tensor_tensor(t, r, r, ALU.mult))
                chain(dve.scalar_tensor_tensor(out=t, in0=t, scalar=-0.5, in1=var, op0=ALU.mult, op1=ALU.mult))
                chain(dve.scalar_tensor_tensor(out=dst, in0=t, scalar=1.5, in1=r, op0=ALU.add, op1=ALU.mult))

            def scale_mixer(m, y, k, k_set=0):
                r = SETS[k_set][1]
                inv_root(k, r, k_set)
                for b in range(NG):
                    dve.scalar_tensor_tensor(out=y[:, b, :], in0=y[:, b, :], scalar=v("out_norm_g", m * NG + b),
                                             in1=r, op0=ALU.mult, op1=ALU.mult).then_inc(scaled[m], 1)

            def mixer_lo(m, y):
                for b in range(NG):
                    dve.wait_ge(mix_hi[m], b + 1)
                    dve.tensor_tensor(ML[:, m * NG + b, :], y[:, b, :], MH[:, m * NG + b, :].bitcast(F32),
                                      ALU.subtract).then_inc(mix_lo[m], 1)

            def conv_taps(n):
                for k in range(taps_done[0], taps_done[0] + n):
                    for b in range(NG):
                        for h in range(2):
                            i = (k * NG + b) * 2 + h
                            src, acc = g_at(b, k)[h], two(T1[:, b, :])[h]
                            if k == 0:
                                ins = dve.tensor_scalar(acc, src, tap(0, b), v("conv_a_b", b), ALU.mult, ALU.add)
                            else:
                                dve.wait_ge(conv_done, i - 2 * NG + 1)
                                ins = dve.scalar_tensor_tensor(out=acc, in0=src, scalar=tap(k, b), in1=acc,
                                                               op0=ALU.mult, op1=ALU.add)
                            ins.then_inc(conv_done, 1)
                taps_done[0] += n

            def pooling(b):
                w = 2 << b
                src, width = PP[:, b, :], 1
                if b:
                    dve.wait_ge(pooled, b)
                for level in range(b + 1):
                    dst = (S_A, S_B)[level % 2]
                    start = 2 * width - 1
                    chain(dve.tensor_tensor(dst[:, start:PL], src[:, start:PL], src[:, start - width:PL - width], ALU.add))
                    src, width = dst, 2 * width
                assert width == w
                sums_at = (src[:, PW:PA], src[:, PA:PL].rearrange("p (s r) -> p s r", s=NB)[:, :, PW:PS])
                for h in range(2):
                    ins = dve.scalar_tensor_tensor(out=two(T2[:, b, :])[h], in0=sums_at[h], scalar=1.0 / w,
                                                   in1=p_at(b, PW)[h], op0=ALU.mult, op1=ALU.subtract)
                    chain(ins)
                head = sums_at[0][:, 0:w - 1]
                chain(dve.tensor_tensor(head, head, inv[:, 0:w - 1], ALU.mult))
                dve.tensor_tensor(T2[:, b, 0:w - 1], head, PP[:, b, PW:PW + w - 1], ALU.subtract).then_inc(pooled, 1)

            def residual(b, src):
                dve.tensor_tensor(X[:, b, :], src[:, 0:T], X[:, b, :], ALU.add).then_inc(banks_free, 1)

            def silu(count):
                for n in range(NG):
                    dve.wait_ge(ffn_sig, count + n + 1)
                    dve.tensor_tensor(SG[:, n, :], SG[:, n, :], T0[:, n, :], ALU.mult).then_inc(ffn_silu, 1)
                for n in range(NG):
                    dve.wait_ge(ffn_silu, count + n + 1)
                    dve.tensor_tensor(SG[:, n, :], SG[:, n, :], s_bc[:, :], ALU.mult).then_inc(ffn_scaled, 1)

            for b in range(KD):
                dve.wait_ge(banks_full, b + 1)
                dve.tensor_copy(X[:, b, :], bank[b % BANKS][:, 0:T]).then_inc(banks_free, 1)
                if b == 0:
                    dve.wait_ge(misc_act, 1)
                if b >= 2:
                    x_part(b - 2)
                if b in (5, 7, 9):
                    lo_at((b - 5) // 2)
            x_part(KD - 2)
            x_part(KD - 1)

            for t in range(T_LOOP):
                lo_at(t + AHEAD)
                if t in TAPS:
                    if t == 16:
                        dve.wait_ge(glu_ready, NG)
                        dve.wait_ge(banks_free, use_of(1, NG - 1) + 1)
                        dve.wait_ge(misc_act, ACT_COUNT["st_c"])
                        dve.wait_ge(pads_ready, 4)
                    conv_taps(TAPS[t])
                if t == 6:
                    var_out("s1")
                if t == 7:
                    inv_root(NORM["s1"], s_bc[:, :])
                    for n in range(NG):
                        src = in_block(0, n)
                        dve.tensor_tensor(T0[:, n, :], src[:, 0:T], s_bc[:, :], ALU.mult).then_inc(banks_free, 1)
                if t == 9:
                    for n in range(NG):
                        dve.wait_ge(gate_sig, n + 1)
                        chain(dve.tensor_tensor(T0[:, n, :], T0[:, n, :], s_bc[:, :], ALU.mult))
                if t == 15:
                    for n in range(NG):
                        src, dst, sig = two(in_block(1, n)[:, 0:T]), g_at(n, CW - 1), two(T0[:, n, :])
                        dve.tensor_tensor(dst[0], src[0], sig[0], ALU.mult).then_inc(glu_ready, 1)
                        dve.tensor_tensor(dst[1], src[1], sig[1], ALU.mult).then_inc(banks_free, 1)
                if t == 23:
                    for n in range(NG):
                        src, dst, s = two(in_block(2, n)[:, 0:T]), p_at(n, PW), two(s_bc[:, :])
                        dve.tensor_tensor(dst[0], src[0], s[0], ALU.mult).then_inc(pin_ready, 1)
                        dve.tensor_tensor(dst[1], src[1], s[1], ALU.mult).then_inc(banks_free, 1)
                if t == 24:
                    dve.wait_ge(banks_free, use_of(2, NG - 1) + 1)
                    dve.wait_ge(misc_act, ACT_COUNT["st_p"])
                    pooling(0)
                    pooling(1)
                if t == 25:
                    pooling(2)
                if t == 26:
                    pooling(3)
                if t == 29:
                    var_out("b_rms")
                if t == 30:
                    scale_mixer(MIX_B, T2, NORM["b_rms"])
                if t == 31:
                    mixer_lo(MIX_B, T2)
                    for n in range(NG):
                        src = in_block(3, n)
                        dve.tensor_tensor(T0[:, n, :], src[:, 0:T], s_bc[:, :], ALU.mult).then_inc(banks_free, 1)
                if t == 33:
                    dve.wait_ge(misc_full, MISC_AT["d_mean"] + 1)
                    for n in range(NG):
                        dve.tensor_tensor(T0[:, n, :], T0[:, n, :], misc_bank("d_mean")[:, 0:T],
                                          ALU.subtract).then_inc(d_cent, 1)
                if t == 35:
                    var_out("d_var")
                if t == 36:
                    r = SETS[0][1]
                    inv_root(NORM["d_var"], r)
                    for n in range(NG):
                        dve.tensor_tensor(T0[:, n, :], T0[:, n, :], r, ALU.mult).then_inc(d_unit, 1)
                if t == 39:
                    dve.wait_ge(b_stored, 32)
                    for n in range(NG):
                        src = in_block(4, n)
                        dve.tensor_tensor(T4[:, n, :], src[:, 0:T], s_bc[:, :], ALU.mult).then_inc(banks_free, 1)
                if 40 <= t <= 41:
                    for n in (0, 1) if t == 40 else (2, 3):
                        dve.wait_ge(banks_free, use_of(4, n) + 1)
                        dve.wait_ge(misc_full, MISC_AT[f"z{n}"] + 1)
                        dve.tensor_tensor(T4[:, n, :], misc_bank(f"z{n}")[:, 0:T], T4[:, n, :],
                                          ALU.mult).then_inc(d_out, 1)
                if t == 43:
                    var_out("d_rms")
                if t == 44:
                    scale_mixer(MIX_D, T4, NORM["d_rms"])
                if t == 45:
                    mixer_lo(MIX_D, T4)
                if t == 47:
                    dve.wait_ge(misc_full, MISC_AT["vt2"] + 1)
                    for n in range(NG):
                        src = in_block(5, n)
                        dve.tensor_tensor(T0[:, n, :], src[:, 0:T], s_bc[:, :], ALU.mult).then_inc(banks_free, 1)
                if t == 48:
                    for n in range(NG):
                        dve.wait_ge(banks_free, use_of(5, n) + 1)
                        chain(dve.tensor_tensor(T0[:, n, :], T0[:, n, :], s_bc[:, :], ALU.mult))
                if t == 55:
                    for n in range(NG):
                        src, dst, ch = two(in_block(6, n)[:, 0:T]), c_at(n, SW - 1), two(T0[:, n, :])
                        dve.tensor_tensor(dst[0], src[0], ch[0], ALU.mult).then_inc(cin_ready, 1)
                        dve.tensor_tensor(dst[1], src[1], ch[1], ALU.mult).then_inc(banks_free, 1)
                if t == 56:
                    dve.wait_ge(banks_free, use_of(6, NG - 1) + 1)
                if t in (56, 57):
                    bs = (0, 1) if t == 56 else (2, 3)
                    for k in range(SW):
                        for b in bs:
                            for h in range(2):
                                src, acc, w = c_at(b, k)[h], two(T2[:, b, :])[h], v("sconv_w", k * NG + b)
                                if k == 0:
                                    ins = dve.tensor_scalar(acc, src, w, None, ALU.mult)
                                else:
                                    ins = dve.scalar_tensor_tensor(out=acc, in0=src, scalar=w, in1=acc,
                                                                   op0=ALU.mult, op1=ALU.add)
                                if (b, h) == (bs[-1], 1):
                                    chain(ins)
                    for b in bs:
                        chain(dve.tensor_tensor(T2[:, b, :], T2[:, b, :], s_bc[:, :], ALU.mult))
                if t == 59:
                    dve.wait_ge(misc_full, MISC_AT["a_mean"] + 1)
                    for n in range(NG):
                        dve.tensor_tensor(T1[:, n, :], T1[:, n, :], misc_bank("a_mean")[:, 0:T],
                                          ALU.subtract).then_inc(a_cent, 1)
                if t == 61:
                    var_out("a_var", 1)
                if t == 62:
                    r = SETS[1][1]
                    inv_root(NORM["a_var"], r, 1)
                    for n in range(NG):
                        dve.tensor_tensor(T1[:, n, :], T1[:, n, :], r, ALU.mult).then_inc(a_unit, 1)
                if t == 63:
                    for n in range(NG):
                        src = in_block(7, n)
                        ins = dve.tensor_tensor(T2[:, n, :], src[:, 0:T], T2[:, n, :], ALU.mult)
                        ins.then_inc(banks_free, 1)
                if t == 64:
                    for n in range(NG):
                        dve.wait_ge(a_act, n + 1)
                        dve.tensor_tensor(T1[:, n, :], T1[:, n, :], SG[:, n, :], ALU.mult).then_inc(a_out, 1)
                if t == 65:
                    var_out("c_rms")
                if t == 66:
                    scale_mixer(MIX_C, T2, NORM["c_rms"])
                    var_out("a_rms", 1)
                if t == 67:
                    mixer_lo(MIX_C, T2)
                    scale_mixer(MIX_A, T1, NORM["a_rms"], 1)
                if t == 68:
                    mixer_lo(MIX_A, T1)
                if T_OUT <= t < T_G0 and t % PER == PER - 1:
                    for n in range(NG):
                        s = (t - T_OUT) // PER
                        residual(s * NG + n, strip_block(S_OUT + s, n, t))
                if T_OUT < t <= T_G0 and t % PER == 0:
                    for b in range((t - T_OUT) // PER * NG - NG, (t - T_OUT) // PER * NG):
                        dve.wait_ge(y_hi, b + 1)
                        dve.scalar_tensor_tensor(out=XL[:, b, :], in0=X[:, b, :], scalar=v("norm_ffn_g", b),
                                                 in1=XH[:, b, :].bitcast(F32), op0=ALU.mult,
                                                 op1=ALU.subtract).then_inc(y_lo, 1)
                if t == T_G0 + 4:
                    var_out("s2")
                if t == T_G0 + 5:
                    inv_root(NORM["s2"], s_bc[:, :])
                if t == T_U0 - 1:
                    for n in range(NG):
                        src = strip_block(S_G0, n, t)
                        dve.tensor_tensor(SG[:, n, :], src[:, 0:T], s_bc[:, :], ALU.mult).then_inc(banks_free, 1)
                if t == T_U0 + 1:
                    silu(0)
                if t == T_LOOP - 1:
                    dve.wait_ge(ffn_scaled, NG)
                    for n in range(NG):
                        src = strip_block(S_U0, n, t)
                        dve.tensor_tensor(HU[:, n, :], src[:, 0:T], SG[:, n, :], ALU.mult).then_inc(banks_free, 1)

            def hidden_lo(count):
                for b in range(NG):
                    dve.wait_ge(h_hi, count + b + 1)
                    dve.tensor_tensor(ML[:, b, :], HU[:, b, :], MH[:, b, :].bitcast(F32), ALU.subtract).then_inc(h_lo, 1)

            with dve.Fori(0, NF - 1) as g:
                def loop_block(i, n, j):
                    if n < NG - 1:
                        dve.wait_ge(banks_full, g * ((NG - 1) * S_BODY) + full_at(S_LOOP + i, n))
                    else:
                        dve.wait_ge(tile_used, g * BODY + (T_LOOP + j + 1))
                    return bank[use_of(S_LOOP + i, n) % BANKS]

                for j in range(BODY):
                    t = T_LOOP + j + AHEAD
                    lo(t, g * BODY + (t + 1))
                    if j == 0:
                        hidden_lo(g * NG)
                    if j == PER - 1:
                        for n in range(NG):
                            src = loop_block(0, n, j)
                            dve.tensor_tensor(SG[:, n, :], src[:, 0:T], s_bc[:, :], ALU.mult).then_inc(banks_free, 1)
                    if PER < j < BODY - PER and j % PER_DN == PER_DN - 1:
                        s = (j - PER) // PER_DN
                        for n in range(NG):
                            residual(s * NG + n, loop_block(1 + s, n, j))
                    if j == PER + 2:
                        silu(g * NG + NG)
                    if j == BODY - 1:
                        dve.wait_ge(ffn_scaled, g * NG + 2 * NG)
                        for n in range(NG):
                            src = loop_block(S_BODY - 1, n, j)
                            dve.tensor_tensor(HU[:, n, :], src[:, 0:T], SG[:, n, :], ALU.mult).then_inc(banks_free, 1)
            for t in range(T_END, TILES):
                lo_at(t + AHEAD)
                if t == T_END:
                    hidden_lo((NF - 1) * NG)
                if (t - T_END) % PER_DN == PER_DN - 1:
                    s = (t - T_END) // PER_DN
                    for n in range(NG):
                        residual(s * NG + n, strip_block(S_END + s, n, t))

            var, sd, tmp, r = (norm0[:, 3 * i:3 * i + 3] for i in range(4))
            dve.wait_ge(misc_full, MISC_AT["s3"] + 1)
            for n, c0, c1 in Y_PARTS:
                ins = dve.tensor_scalar(var[0:n, c0:c1], misc_bank("s3")[0:n, c0:c1], EPS, None, ALU.add)
            ins.then_inc(var_ready, 1)
            dve.wait_ge(sd_ready, NORM["s3"] + 1)
            for n, c0, c1 in Y_PARTS:
                v_, s_, t_, r_ = (x[0:n, c0:c1] for x in (var, sd, tmp, r))
                chain(dve.reciprocal(s_, s_))
                chain(dve.tensor_tensor(t_, s_, s_, ALU.mult))
                chain(dve.scalar_tensor_tensor(out=t_, in0=t_, scalar=-0.5, in1=v_, op0=ALU.mult, op1=ALU.mult))
                ins = dve.scalar_tensor_tensor(out=r_, in0=t_, scalar=1.5, in1=s_, op0=ALU.add, op1=ALU.mult)
            ins.then_inc(r_ready, 1)
            dve.wait_ge(r_ready, 1)
            dve.wait_ge(c_stored, 32)
            for w in range(0, 3 * NG, 2):
                c, q = divmod(w, NG)
                n = P if c < 2 else NB * NS
                dve.wait_ge(banks_full, full_at(S_ALL, 0) + w)
                dve.tensor_scalar(y_rows(c, q)[0:n, :], bank[(use_of(S_ALL, 0) + w) % BANKS][0:n, :],
                                  r[0:n, c:c + 1], None, ALU.mult).then_inc(out_dve, 1)

        @block.tensor
        def _(pe):
            def into(name):
                i = MISC_AT[name]
                if i >= 2:
                    s, count = TAKEN[MISC[i - 2]]
                    pe.wait_ge(SEMS[s], count)
                return misc_bank(name)

            def sum_over(name, weights, src):
                M = into(name)
                for b in range(NG):
                    last = pe.matmul(M[:, 0:T], weights[:, :], src[:, b, :], start=(b == 0), stop=(b == NG - 1))
                last.then_inc(misc_full, 1)

            def turn(name, parts):
                for out, in_ in parts:
                    k = in_.shape[0]
                    last = pe.transpose(out, in_, ident[0:k, 0:k])
                last.then_inc(misc_full, 1)

            def products(t, banks, moving, first, last, free_count, moving_ready=None):
                W_H, W_L = (slot(x, t).rearrange("p (k n) -> p k n", k=TK) for x in (wh, wl))
                if moving_ready is not None:
                    pe.wait_ge(*moving_ready)
                for n in range(NG):
                    if first:
                        pe.wait_ge(banks_free, free_count + n)
                    for k in range(TK):
                        hi_, lo_ = moving(k)
                        cols = slice(n * P, (n + 1) * P)
                        pe.matmul(banks[n][:, 0:T], W_H[:, k, cols], hi_, start=(first and k == 0), stop=False)
                        pe.matmul(banks[n][:, 0:T], W_H[:, k, cols], lo_, start=False, stop=False)
                        mm = pe.matmul(banks[n][:, 0:T], W_L[:, k, cols], hi_, start=False, stop=(last and k == TK - 1))
                    if last and n < NG - 1:
                        mm.then_inc(banks_full, 1)
                mm.then_inc(tile_used, 1)

            def strip_banks(strip):
                return [bank[use_of(strip, n) % BANKS] for n in range(NG)]

            def tile(t, strip, kt, tiles, xh, xl, base, moving_ready=None):
                pe.wait_ge(lo_ready, t + 1)
                products(t, strip_banks(strip), lambda k: (xh[:, base + k, :], xl[:, base + k, :]), kt == 0,
                         kt == tiles - 1, use_of(strip, 0) - BANKS + 1, moving_ready)

            pe.wait_ge(const_ready, 4)
            pe.wait_ge(vecs_landed, 16 * (len(VECS) + 1))
            M = misc_bank("vecs")
            turn("vecs", [(M[:, 0:NV], vec_rows[0:NV, :]), (M[:, P:P + CW * NG], tap_rows[0:CW * NG, :])])
            for b in range(KD):
                if b >= BANKS:
                    pe.wait_ge(banks_free, b - BANKS + 1)
                cols = slice(b * P, (b + 1) * P)
                for c in range(3):
                    if b == 0:
                        pe.wait_ge(x_landed[c], 16)
                    n = P if c < 2 else NB * NS
                    last = pe.transpose(bank[b % BANKS][:, c * P:c * P + n], stage[0:n, c, cols], ident[0:n, 0:n])
                last.then_inc(banks_full, 1)

            for t in range(T_LOOP):
                if t < T_OUT:
                    s, kt = divmod(t, PER)
                    tile(t, s, kt, PER, XH, XL, kt * TK, (x_lo, kt * TK + TK) if s == 0 else None)
                elif t < T_G0:
                    s, kt = divmod(t - T_OUT, PER)
                    m, half = OUT_ORDER[kt // 2], kt % 2
                    tile(t, S_OUT + s, kt, PER, MH, ML, m * NG + half * TK,
                         (mix_lo[m], half * TK + TK) if s == 0 else None)
                else:
                    s, kt = divmod(t - T_G0, PER)
                    tile(t, S_G0 + s, kt, PER, XH, XL, kt * TK, (y_lo, kt * TK + TK) if s == 0 else None)
                if t == 1:
                    pe.wait_ge(sgu_landed, 16)
                    turn("sgu_w", [(into("sgu_w")[:, g * P:(g + 1) * P], sgu_rows[:, g * P:(g + 1) * P]) for g in range(NG)])
                if t == 5:
                    M = into("s1")
                    pe.wait_ge(sums, 1)
                    pe.matmul(M[:, 0:T], ones_d[:, :], sum_sq[:, :], start=True, stop=True).then_inc(misc_full, 1)
                if 8 <= t <= 9:
                    for b in (0, 1) if t == 8 else (2, 3):
                        pe.wait_ge(late_landed, 48)
                        M, half = into(f"st_a{b}"), NB // 2 * (CW - 1)
                        turn(f"st_a{b}", [(M[:, h * half:(h + 1) * half], st_a[0:half, h, b * P:(b + 1) * P]) for h in range(2)])
                if t == 10:
                    M = into("st_p")
                    turn("st_p", [(M[:, b * P:b * P + NB * PW], st_p[0:NB * PW, b * P:(b + 1) * P]) for b in range(NG)])
                    M = into("st_c")
                    turn("st_c", [(M[:, b * P:b * P + NB * (SW - 1)], st_c[0:NB * (SW - 1), b * P:(b + 1) * P]) for b in range(NG)])
                if t == 17:
                    pe.wait_ge(banks_free, use_of(1, NG - 1) + 1)
                    M = into("new_ap")
                    turn("new_ap", [(M[0:CW - 1, b * P:(b + 1) * P], G[:, b, SEQ:GA]) for b in range(NG)])
                    pe.wait_ge(tails_ready, 1)
                    M = into("new_as")
                    turn("new_as", [(M[0:NB * NS, b * P:(b + 1) * P], tails[:, b * NB * NS:(b + 1) * NB * NS]) for b in range(NG)])
                if t == 24:
                    pe.wait_ge(banks_free, use_of(2, NG - 1) + 1)
                    M = into("new_pp")
                    turn("new_pp", [(M[0:PW, b * P:(b + 1) * P], PP[:, b, SEQ:PA]) for b in range(NG)])
                    pe.wait_ge(tails_ready, 2)
                    M = into("new_ps")
                    turn("new_ps", [(M[0:NB * NS, b * P:(b + 1) * P], tails[:, b * NB * NS:(b + 1) * NB * NS]) for b in range(NG)])
                if 26 <= t <= 27:
                    for b in (0, 1) if t == 26 else (2, 3):
                        M = into(f"b{b}")
                        pe.wait_ge(pooled, b + 1)
                        if b == 0:
                            pe.wait_ge(mats_landed, 32)
                        pe.matmul(M[:, 0:T], PWV[:, b, :], T2[:, b, :], start=True, stop=True).then_inc(misc_full, 1)
                if t == 28:
                    pe.wait_ge(squares, NG)
                    sum_over("b_rms", ones_g, SQ)
                if t == 32:
                    pe.wait_ge(banks_free, use_of(3, NG - 1) + 1)
                    sum_over("d_mean", ones_g, T0)
                if t == 34:
                    pe.wait_ge(squares, 2 * NG)
                    sum_over("d_var", ones_g, SQ)
                if 37 <= t <= 38:
                    pe.wait_ge(vn_ready, NG)
                    for c in (0, 1) if t == 37 else (2,):
                        M, n = into(f"vt{c}"), P if c < 2 else NB * NS
                        turn(f"vt{c}", [(M[0:n, b * P:(b + 1) * P], T0[:, b, c * P:c * P + n]) for b in range(NG)])
                if 39 <= t <= 40:
                    pe.wait_ge(misc_act, ACT_COUNT["vt2"])
                    pe.wait_ge(masked, 1)
                    pe.wait_ge(corner_landed, 16 * NB)
                    for b in (0, 1) if t == 39 else (2, 3):
                        M, cols = into(f"z{b}"), slice(b * P, (b + 1) * P)
                        for c in range(2):
                            out = M[:, c * P:(c + 1) * P]
                            pe.matmul(out, vt[:, c, cols], WT[:, b, :], start=True, stop=False)
                            pe.matmul(out, ones[0:1, :], BROW[:, b, :], start=False, stop=True)
                        out = M[:, SEQ:T]
                        pe.matmul(out, vt[0:NB * NS, 2, cols], BD[:, b, :], start=True, stop=False)
                        bias = BROW[:, b, 0:NS].unsqueeze(1).to_broadcast([1, NB, NS])
                        pe.matmul(out, ones[0:1, :], bias, start=False, stop=True).then_inc(misc_full, 1)
                if t == 42:
                    pe.wait_ge(squares, 3 * NG)
                    sum_over("d_rms", ones_g, SQ)
                if t == 56:
                    pe.wait_ge(banks_free, use_of(6, NG - 1) + 1)
                    M = into("new_cp")
                    turn("new_cp", [(M[0:SW - 1, b * P:(b + 1) * P], C[:, b, SEQ:CA]) for b in range(NG)])
                    pe.wait_ge(tails_ready, 3)
                    M = into("new_cs")
                    turn("new_cs", [(M[0:NB * (SW - 1), b * P:(b + 1) * P], tails[:, b * NB * (SW - 1):(b + 1) * NB * (SW - 1)]) for b in range(NG)])
                if t == 58:
                    pe.wait_ge(conv_done, CW * NG * 2)
                    sum_over("a_mean", ones_g, T1)
                if t == 60:
                    pe.wait_ge(squares, 4 * NG)
                    sum_over("a_var", ones_g, SQ)
                if t == 64:
                    pe.wait_ge(squares, 5 * NG)
                    sum_over("c_rms", ones_g, SQ)
                if t == 65:
                    pe.wait_ge(squares, 6 * NG)
                    sum_over("a_rms", ones_g, SQ)
                if t == T_G0 + 3:
                    M = into("s2")
                    pe.wait_ge(sums, 2)
                    pe.matmul(M[:, 0:T], ones_d[:, :], sum_sq[:, :], start=True, stop=True).then_inc(misc_full, 1)

            with pe.Fori(0, NF - 1) as g:
                for j in range(BODY):
                    t = T_LOOP + j
                    down = PER <= j < BODY - PER
                    if down:
                        i, kt = (j - PER) // PER_DN + 1, (j - PER) % PER_DN
                        tiles, xh, xl, base = PER_DN, MH, ML, kt * TK
                    else:
                        i, kt = (0, j) if j < PER else (S_BODY - 1, j - (BODY - PER))
                        tiles, xh, xl, base = PER, XH, XL, kt * TK
                    pe.wait_ge(lo_ready, g * BODY + (t + 1))
                    products(t, strip_banks(S_LOOP + i), lambda k: (xh[:, base + k, :], xl[:, base + k, :]), kt == 0,
                             kt == tiles - 1, g * (NG * S_BODY) + (use_of(S_LOOP + i, 0) - BANKS + 1),
                             (h_lo, g * NG + NG) if j == PER else None)
            for t in range(T_END, TILES):
                s, kt = divmod(t - T_END, PER_DN)
                tile(t, S_END + s, kt, PER_DN, MH, ML, kt * TK, (h_lo, (NF - 1) * NG + kt * TK + TK) if s == 0 else None)

            M = into("s3")
            pe.wait_ge(sums, 3)
            for c in range(3):
                n = P if c < 2 else NB * NS
                last = pe.matmul(M[0:n, c:c + 1], sum_sq[:, c * P:c * P + n], ones_d[:, 0:1], start=True, stop=True)
            last.then_inc(misc_full, 1)
            for w in range(3 * NG):
                c, q = divmod(w, NG)
                n = P if c < 2 else NB * NS
                if w < BANKS:
                    pe.wait_ge(banks_free, use_of(S_ALL, 0) + w - BANKS + 1)
                else:
                    pe.wait_ge(out_dve if w % 2 == 0 else out_act, (w - BANKS) // 2 + 1)
                for b in range(q * NG, (q + 1) * NG):
                    pe.wait_ge(out_scaled, b + 1)
                    last = pe.transpose(bank[(use_of(S_ALL, 0) + w) % BANKS][0:n, (b % NG) * P:(b % NG + 1) * P],
                                        X[:, b, c * P:c * P + n], ident[:, :])
                last.then_inc(banks_full, 1)


_INS = ["x_prompt", "x_sample", "state_conv_a", "state_pool", "state_sconv", "norm_mix_g", "w_in", "conv_a_w",
        "conv_a_b", "ln_a_g", "ln_a_b", "pool_w", "pool_scale", "sconv_w", "sgu_ln_g", "sgu_ln_b", "sgu_w",
        "sgu_b", "out_norm_g", "w_out", "norm_ffn_g", "w_gate", "w_up", "w_down", "final_norm_g"]
_OUTS = [(1, SEQ, D), (NB, NS, D), (1, 1, CW - 1, GRP), (1, NB, CW - 1, GRP), (1, 1, PW, GRP), (1, NB, PW, GRP),
         (1, 1, SW - 1, GRP), (1, NB, SW - 1, GRP), (1, NB, NS, GRP)]


def kernel(**inputs):
    import numpy as np
    import concourse.bacc as bacc
    from concourse.bass_utils import run_bass_kernel_spmd

    nc = bacc.Bacc("TRN2", target_bir_lowering=False, num_devices=1)
    arrays, aps = {}, {}
    for name in _INS:
        x = np.ascontiguousarray(inputs[name])
        arrays[f"in_{name}"] = x
        ap = nc.dram_tensor(f"in_{name}", x.shape, mybir.dt.from_np(x.dtype), kind="ExternalInput").ap()
        aps[name] = ap if name in ("x_prompt", "x_sample", "final_norm_g") else ap[0]
    aps["sconv_w"] = aps["sconv_w"].rearrange("k c -> (k c)")
    outs = [nc.dram_tensor(f"out_{i}", s, F32, kind="ExternalOutput").ap() for i, s in enumerate(_OUTS)]
    hybrid_step(nc, aps, outs)
    r = run_bass_kernel_spmd(nc, [arrays], core_ids=[0])
    return tuple(r.results[0][f"out_{i}"] for i in range(len(_OUTS)))
```

```python
from contextlib import ExitStack

import concourse.bass as bass
from concourse import mybir
from concourse.alu_op_type import AluOpType as ALU

ACT = mybir.ActivationFunctionType
F32 = mybir.dt.float32
F32R = mybir.dt.float32r

P = 128
D = 2048
KD = D // P
SEQ = 256
NB, NS = 8, 4
T = SEQ + NB * NS
GRP = 512
NG = GRP // P
F = 5632
NF = F // GRP
CW = 31
PW = 15
SW = 3
EPS = 1e-6

TK = 2
TILE = TK * GRP
RING = 4
BANKS = 6
XQ = 4
AHEAD = RING - 1

GA, GS = CW - 1 + SEQ, CW - 1 + NS
PA, PS = PW + SEQ, PW + NS
CA, CS = SW - 1 + SEQ, SW - 1 + NS
GL, PL, CL = GA + NB * GS, PA + NB * PS, CA + NB * CS

A_VAL, A_GATE, POOL, C_H, C_B, C_C, D_U, D_V = range(8)
STRIPS = [A_GATE, A_VAL, POOL, D_V, D_U, C_H, C_C, C_B]
MIX_A, MIX_B, MIX_C, MIX_D = range(4)
OUT_ORDER = [MIX_B, MIX_D, MIX_A, MIX_C]

PER = D // (TK * P)
T_IN = 0
T_OUT = T_IN + len(STRIPS) * PER
T_G0 = T_OUT + (D // GRP) * PER
T_U0 = T_G0 + PER
T_LOOP = T_U0 + PER
PER_DN = GRP // (TK * P)
BODY = 2 * PER + (D // GRP) * PER_DN
T_END = T_LOOP + (NF - 1) * BODY
TILES = T_END + (D // GRP) * PER_DN

S_OUT = len(STRIPS)
S_G0 = S_OUT + D // GRP
S_U0 = S_G0 + 1
S_LOOP = S_U0 + 1
S_BODY = 2 + D // GRP
S_END = S_LOOP + (NF - 1) * S_BODY
S_ALL = S_END + D // GRP
assert S_BODY * NG % BANKS == 0 and BODY % RING == 0

VECS = [("norm_mix_g", KD), ("conv_a_b", NG), ("ln_a_g", NG), ("ln_a_b", NG), ("pool_scale", NG),
        ("sgu_ln_g", NG), ("sgu_ln_b", NG), ("out_norm_g", KD), ("norm_ffn_g", KD), ("final_norm_g", KD),
        ("sconv_w", SW * NG), ("conv_a_w", CW * NG)]
VROW, NV = {}, 0
for _name, _rows in VECS:
    VROW[_name] = NV
    NV += _rows

NORM = {n: i for i, n in enumerate(["s1", "b_rms", "d_var", "d_rms", "a_var", "a_rms", "c_rms", "s2", "s3"])}
TAKEN = {n: ("var_ready", i + 1) for n, i in NORM.items()}
TAKEN.update({"d_mean": ("d_cent", NG), "a_mean": ("a_cent", NG)})
TAKEN.update({f"b{n}": ("b_out", n + 1) for n in range(NG)})
TAKEN.update({f"vt{n}": ("vt_ready", n + 1) for n in range(3)})
TAKEN.update({f"z{n}": ("d_out", n + 1) for n in range(NG)})
MISC = ["s1", "b0", "b1", "b2", "b3", "b_rms", "d_mean", "d_var", "vt0", "vt1", "vt2", "z0", "z1", "z2", "z3",
        "d_rms", "a_mean", "a_var", "a_rms", "c_rms", "s2", "s3"]
MISC_AT = {name: i for i, name in enumerate(MISC)}

TAPS = {16: 2, 17: 1, 18: 2, 19: 1, 20: 2, 21: 1, 22: 2, 28: 2, 29: 1, 34: 1, 35: 1, 38: 1, 40: 1, 41: 1, 42: 1,
        43: 1, 46: 1, 49: 2, 50: 1, 51: 2, 52: 1, 53: 2, 54: 1}
VG = NG - 1
assert sum(TAPS.values()) == CW


def full_at(strip, n):
    return (NG - 1) * strip + n + 1


def use_of(strip, n):
    return NG * strip + n


def hybrid_step(nc, a, o):
    ctx = ExitStack()
    with ctx:
        def sb(name, cols, dt=F32):
            return ctx.enter_context(nc.sbuf_tensor(name, [P, cols], dt))

        def sem(name):
            return ctx.enter_context(nc.semaphore(name))

        def blocks(t, n=NG):
            return t.rearrange("p (n t) -> p n t", n=n)

        x_sb = sb("x_sb", KD * T)
        xh_sb, xl_sb = sb("xh_sb", KD * T, F32R), sb("xl_sb", KD * T, F32R)
        mh_sb, ml_sb = sb("mh_sb", KD * T, F32R), sb("ml_sb", KD * T, F32R)
        raw = sb("raw", RING * TILE)
        wh, wl = sb("wh", RING * TILE, F32R), sb("wl", RING * TILE, F32R)
        X = blocks(x_sb[:, :], KD)
        XH, XL = blocks(xh_sb[:, :], KD), blocks(xl_sb[:, :], KD)
        MH, ML = blocks(mh_sb[:, :], KD), blocks(ml_sb[:, :], KD)

        NT = NG * T
        T0, T1, T2, T4 = (blocks(sb(f"work{i}", NT)[:, :]) for i in range(4))
        vt = sb("vt", 3 * GRP)[:, :].rearrange("p (c d) -> p c d", c=3)
        g_sb, p_sb, c_sb = sb("g_sb", NG * GL), sb("p_sb", NG * PL), sb("c_sb", NG * CL)
        G, PP, C = blocks(g_sb[:, :]), blocks(p_sb[:, :]), blocks(c_sb[:, :])
        SG = blocks(g_sb[:, 0:NT])
        HU = blocks(p_sb[:, 0:NT])
        sq_sb = sb("sq_sb", NT)
        SQ = blocks(sq_sb[:, :])
        pair = sb("pair", 3 * T)
        S_A, S_B = pair[:, 0:PL], pair[:, PL:2 * PL]
        norm0 = sb("norm0", 3 * T)
        SETS = [[t[:, i * T:(i + 1) * T] for i in range(3)] for t in (norm0, pair)]
        s_bc = sb("s_bc", T)
        s2_bc = sb("s2_bc", T)
        sum_sq, one_sq = sb("sum_sq", T), sb("one_sq", T)
        prod, prod_s = one_sq[:, 0:SEQ], sum_sq[:, 0:NG * NB * NS]

        ident, ones, ones_d, ones_g = (sb(n, P) for n in ("ident", "ones", "ones_d", "ones_g"))
        vec = sb("vec", NV)
        wt = sb("wt", NG * P)
        bd = sb("bd", NG * NB * NS)
        pw = sb("pw", NG * P)
        brow = sb("brow", NG * P)
        inv = sb("inv", PW + 1)
        WT, BD = blocks(wt[:, :]), blocks(bd[0:NB * NS, :])
        PWV, BROW = blocks(pw[:, :]), blocks(brow[0:1, :])

        def v(name, b):
            return vec[:, VROW[name] + b:VROW[name] + b + 1]

        def tap(k, b):
            return v("conv_a_w", k * NG + b)

        def halves(buf, b, width, first, at, n):
            prompt = buf[:, b, at:at + first]
            sample = buf[:, b, width:].rearrange("p (s r) -> p s r", s=NB)[:, :, at:at + n]
            return prompt, sample

        def g_at(b, k):
            return halves(G, b, GA, SEQ, k, NS)

        def p_at(b, k):
            return halves(PP, b, PA, SEQ, k, NS)

        def c_at(b, k):
            return halves(C, b, CA, SEQ, k, NS)

        def two(t):
            return t[:, 0:SEQ], t[:, SEQ:T].rearrange("p (s r) -> p s r", s=NB)

        bank = [ctx.enter_context(nc.psum_tensor(f"bank{i}", [P, 512], F32)) for i in range(BANKS + 2)]

        raw_landed = [sem(f"raw_landed{i}") for i in range(RING)]
        x_landed = [sem(f"x_landed{i}") for i in range(XQ)]
        vec_landed, sgu_landed, mats_landed, hist_landed, corner_landed = (sem(n) for n in (
            "vec_landed", "sgu_landed", "mats_landed", "hist_landed", "corner_landed"))
        hi_ready, lo_ready, tile_used = sem("hi_ready"), sem("lo_ready"), sem("tile_used")
        banks_full, banks_free = sem("banks_full"), sem("banks_free")
        misc_full, b_out, vt_ready = sem("misc_full"), sem("b_out"), sem("vt_ready")
        x_hi, x_lo, y_hi, y_lo = sem("x_hi"), sem("x_lo"), sem("y_hi"), sem("y_lo")
        const_ready, pads_ready, bd_zero, masked = (sem(n) for n in ("const_ready", "pads_ready", "bd_zero", "masked"))
        sums, pool_chain, dve_chain, act_chain = (sem(n) for n in ("sums", "pool_chain", "dve_chain", "act_chain"))
        var_ready, sd_ready, r_ready = sem("var_ready"), sem("sd_ready"), sem("r_ready")
        gate_sig, glu_ready, conv_done = sem("gate_sig"), sem("glu_ready"), sem("conv_done")
        pin_ready, cin_ready, pooled = sem("pin_ready"), sem("cin_ready"), sem("pooled")
        d_cent, d_unit, vn_ready, d_out = sem("d_cent"), sem("d_unit"), sem("vn_ready"), sem("d_out")
        a_cent, a_unit, a_act, a_out = sem("a_cent"), sem("a_unit"), sem("a_act"), sem("a_out")
        squares = sem("squares")
        scaled = [sem(f"scaled{m}") for m in range(4)]
        mix_hi, mix_lo = [sem(f"mix_hi{m}") for m in range(4)], [sem(f"mix_lo{m}") for m in range(4)]
        conv_s_prod, conv_s_done, conv_p_prod, conv_p_done = (sem(n) for n in (
            "conv_s_prod", "conv_s_done", "conv_p_prod", "conv_p_done"))
        ffn_silu, ffn_scaled = sem("ffn_silu"), sem("ffn_scaled")
        ffn_sig, h_hi, h_lo = sem("ffn_sig"), sem("h_hi"), sem("h_lo")
        a_stored, b_stored, v_stored, c_stored = (sem(n) for n in ("a_stored", "b_stored", "v_stored", "c_stored"))
        last_sq, y_ready, y_stored = sem("last_sq"), sem("y_ready"), sem("y_stored")
        SEMS = {"b_out": b_out, "vt_ready": vt_ready, "var_ready": var_ready, "d_cent": d_cent, "a_cent": a_cent, "d_out": d_out}

        def w_rows(w, row, col):
            return w[row:row + TK * P, col:col + GRP].rearrange("(k p) n -> p k n", k=TK)

        def tile_source(t):
            if t < T_OUT:
                s, kt = divmod(t, PER)
                return w_rows(a["w_in"], kt * TK * P, STRIPS[s] * GRP)
            if t < T_G0:
                s, kt = divmod(t - T_OUT, PER)
                m, half = OUT_ORDER[kt // 2], kt % 2
                return w_rows(a["w_out"], m * GRP + half * TK * P, s * GRP)
            if t < T_U0:
                return w_rows(a["w_gate"], (t - T_G0) * TK * P, 0)
            if t < T_LOOP:
                return w_rows(a["w_up"], (t - T_U0) * TK * P, 0)
            s, kt = divmod(t - T_END, PER_DN)
            return w_rows(a["w_down"], (NF - 1) * GRP + kt * TK * P, s * GRP)

        def loop_source(g, j):
            if j < PER or j >= BODY - PER:
                w, kt = (a["w_gate"], j) if j < PER else (a["w_up"], j - (BODY - PER))
                return w[kt * TK * P:(kt + 1) * TK * P, bass.ds(g * GRP + GRP, GRP)].rearrange("(k p) n -> p k n", k=TK)
            s, kt = divmod(j - PER, PER_DN)
            return w_down_rows(g, kt)[:, :, s * GRP:(s + 1) * GRP]

        def w_down_rows(g, kt):
            return a["w_down"][bass.ds(g * GRP + kt * TK * P, TK * P), :].rearrange("(k p) n -> p k n", k=TK)

        def slot(buf, t):
            return buf[:, (t % RING) * TILE:(t % RING + 1) * TILE]

        class Chain:
            def __init__(self, eng, s):
                self.eng, self.s, self.n = eng, s, 0

            def __call__(self, ins):
                self.n += 1
                ins.then_inc(self.s, 1)
                self.eng.wait_ge(self.s, self.n)

        def misc_bank(name):
            return bank[BANKS + MISC_AT[name] % 2]

        block = ctx.enter_context(nc.Block())

        @block.sync
        def _(sp):
            def load(t, src, lo_count, landed_in):
                if lo_count is not None:
                    sp.wait_ge(lo_ready, lo_count)
                sp.dma_start(slot(raw, t).rearrange("p (k n) -> p k n", k=TK), src).then_inc(raw_landed[landed_in], 16)

            for q in range(XQ):
                bs = slice(q * KD // XQ, (q + 1) * KD // XQ)
                sp.dma_start(X[:, bs, :], a["x"][:, bs, :]).then_inc(x_landed[q], 16)
                load(q, tile_source(q), None, q)
            for t in range(XQ, T_LOOP):
                load(t, tile_source(t), t - RING + 1 if t >= RING else None, t % RING)
            with sp.Fori(0, NF - 1) as g:
                for j in range(BODY):
                    t = T_LOOP + j
                    load(t, loop_source(g, j), g * BODY + (t - RING + 1), t % RING)
            for t in range(T_END, TILES):
                load(t, tile_source(t), t - RING + 1, t % RING)

            for b in range(KD):
                sp.wait_ge(y_ready, b + 1)
                sp.dma_start(o["y"][:, b, :], X[:, b, :]).then_inc(y_stored, 16)
            sp.wait_ge(y_stored, 16 * KD)
            sp.wait_ge(a_stored, 16)
            sp.wait_ge(b_stored, 16)
            sp.wait_ge(v_stored, 16)
            sp.wait_ge(c_stored, 16)

        @block.gpsimd
        def _(pool):
            chain = Chain(pool, pool_chain)
            chain(pool.memset(ident[:, :], 0.0))
            pool.affine_select(out=ident[:, :], in_=ident[:, :], compare_op=ALU.not_equal, fill=1.0, base=0,
                               pattern=[[-1, P]], channel_multiplier=1).then_inc(const_ready, 1)
            pool.memset(ones[:, :], 1.0).then_inc(const_ready, 1)
            pool.memset(ones_d[:, :], 1.0 / D).then_inc(const_ready, 1)
            pool.memset(ones_g[:, :], 1.0 / GRP).then_inc(const_ready, 1)
            pool.memset(bd[0:NB * NS, :], 0.0).then_inc(bd_zero, 1)
            pool.memset(G[:, :, 0:CW - 1], 0.0).then_inc(pads_ready, 1)
            pool.memset(PP[:, :, 0:PW], 0.0).then_inc(pads_ready, 1)
            pool.memset(C[:, :, 0:SW - 1], 0.0).then_inc(pads_ready, 1)
            for t in range(PW):
                last = pool.memset(inv[:, t:t + 1], 1.0 / (t + 1))
            last.then_inc(pads_ready, 1)

            def sum_squares(b, last):
                if b == 0:
                    chain(pool.tensor_tensor(sum_sq[:, :], X[:, b, :], X[:, b, :], ALU.mult))
                    return
                chain(pool.tensor_tensor(one_sq[:, :], X[:, b, :], X[:, b, :], ALU.mult))
                ins = pool.tensor_tensor(sum_sq[:, :], sum_sq[:, :], one_sq[:, :], ALU.add)
                if b == last:
                    ins.then_inc(sums, 1)
                else:
                    chain(ins)

            for b in range(KD):
                if b % (KD // XQ) == 0:
                    pool.wait_ge(x_landed[b // (KD // XQ)], 16)
                sum_squares(b, KD - 1)

            pool.wait_ge(sgu_landed, 16)
            pool.affine_select(out=WT, in_=WT, compare_op=ALU.is_ge, fill=0.0, base=0,
                               pattern=[[0, NG], [1, P]], channel_multiplier=-1).then_inc(masked, 1)

            gs = G[:, :, GA:].rearrange("p b (s r) -> p b s r", s=NB)
            ys = T1[:, :, SEQ:].rearrange("p b (s r) -> p b s r", s=NB)
            ps = prod_s.rearrange("p (b s r) -> p b s r", b=NG, s=NB)
            pool.wait_ge(misc_full, MISC_AT["s1"] + 1)
            pool.wait_ge(vec_landed, 16)
            pool.wait_ge(banks_free, use_of(1, NG - 1) + 1)
            pool.wait_ge(hist_landed, 48)
            for k in range(CW):
                w = vec[:, VROW["conv_a_w"] + k * NG:VROW["conv_a_w"] + (k + 1) * NG]
                w = w.unsqueeze(2).unsqueeze(3).to_broadcast([P, NG, NB, NS])
                src, acc = G[:, VG, k:k + SEQ], T1[:, VG, 0:SEQ]
                w_last = tap(k, VG).to_broadcast([P, SEQ])
                if k == 0:
                    for b in range(NG):
                        ins = pool.tensor_scalar(ys[:, b], gs[:, b, :, 0:NS], tap(0, b), v("conv_a_b", b), ALU.mult, ALU.add)
                    ins.then_inc(conv_s_done, 1)
                    pool.tensor_scalar(acc, src, tap(0, VG), v("conv_a_b", VG), ALU.mult, ALU.add).then_inc(conv_p_done, 1)
                    continue
                if k > 1:
                    pool.wait_ge(conv_p_done, k)
                pool.tensor_tensor(ps, gs[:, :, :, k:k + NS], w, ALU.mult).then_inc(conv_s_prod, 1)
                pool.tensor_tensor(prod, src, w_last, ALU.mult).then_inc(conv_p_prod, 1)
                pool.wait_ge(conv_s_prod, k)
                pool.wait_ge(conv_s_done, k)
                pool.tensor_tensor(ys, ys, ps, ALU.add).then_inc(conv_s_done, 1)
                pool.wait_ge(conv_p_prod, k)
                pool.wait_ge(conv_p_done, k)
                pool.tensor_tensor(acc, acc, prod, ALU.add).then_inc(conv_p_done, 1)

            for b in range(KD):
                pool.wait_ge(banks_free, use_of(S_OUT + b // NG, b % NG) + 1)
                sum_squares(b, KD - 1)
            pool.wait_ge(misc_full, MISC_AT["s2"] + 1)
            for b in range(KD - NG):
                pool.wait_ge(banks_free, use_of(S_END + b // NG, b % NG) + 1)
                sum_squares(b, KD - NG - 1)

        @block.scalar
        def _(act):
            chain = Chain(act, act_chain)
            act.dma_start(vec[:, :], a["vec"]).then_inc(vec_landed, 16)
            act.dma_start(WT, a["sgu_wt"]).then_inc(sgu_landed, 16)
            for buf, width, name in ((G, GA, "hist_a"), (PP, PA, "hist_p"), (C, CA, "hist_c")):
                act.dma_start(buf[:, :, width:], a[name]).then_inc(hist_landed, 16)
            act.dma_start(PWV, a["pool_w"].rearrange("g c d -> c g d")).then_inc(mats_landed, 16)
            act.dma_start(brow[0:1, :], a["sgu_b"].rearrange("(u g) i -> u (g i)", u=1)).then_inc(mats_landed, 16)

            def hi(t, landed, used):
                act.wait_ge(raw_landed[t % RING], landed)
                if used is not None:
                    act.wait_ge(tile_used, used)
                act.activation(slot(wh, t), slot(raw, t), ACT.Copy).then_inc(hi_ready, 1)

            def hi_at(t):
                if t < TILES:
                    hi(t, 16 * (t // RING + 1), t - RING + 1 if t >= RING else None)

            def square(src, ready, count, prior=None):
                act.wait_ge(ready, count)
                if prior is not None:
                    act.wait_ge(misc_full, MISC_AT[prior] + 1)
                for b in range(NG):
                    act.activation(SQ[:, b, :], src[:, b, :], ACT.Square).then_inc(squares, 1)

            def root(k):
                act.wait_ge(var_ready, k + 1)
                s = SETS[1 if k in (NORM["a_rms"], NORM["a_var"]) else 0]
                act.activation(s[1], s[0], ACT.Sqrt).then_inc(sd_ready, 1)

            def mixer_hi(m, src):
                for b in range(NG):
                    act.wait_ge(scaled[m], b + 1)
                    act.activation(MH[:, m * NG + b, :], src[:, b, :], ACT.Copy).then_inc(mix_hi[m], 1)

            act.wait_ge(vec_landed, 16)
            for b in range(KD):
                if b % (KD // XQ) == 0:
                    act.wait_ge(x_landed[b // (KD // XQ)], 16)
                act.activation(XH[:, b, :], X[:, b, :], ACT.Copy, scale=v("norm_mix_g", b)).then_inc(x_hi, 1)
                if b in (1, 5, 9):
                    hi_at((b - 1) // 4)

            for t in range(T_LOOP):
                hi_at(t + AHEAD)
                if t == 7:
                    root(NORM["s1"])
                if t == 8:
                    for b in range(NG):
                        act.wait_ge(banks_free, use_of(0, b) + 1)
                        act.activation(T0[:, b, :], T0[:, b, :], ACT.Sigmoid).then_inc(gate_sig, 1)
                if t == 12:
                    act.wait_ge(masked, 1)
                    act.wait_ge(bd_zero, 1)
                    for s in range(NB):
                        act.dma_start(BD[s * NS:(s + 1) * NS, :, s * NS:(s + 1) * NS],
                                      WT[0:NS, :, 0:NS]).then_inc(corner_landed, 16)
                if t == 17:
                    act.wait_ge(banks_free, use_of(1, NG - 1) + 1)
                    act.wait_ge(hist_landed, 48)
                    act.dma_start(o["a"], G[:, :, SEQ:]).then_inc(a_stored, 16)
                if t == 24:
                    act.wait_ge(banks_free, use_of(2, NG - 1) + 1)
                    act.dma_start(o["p"], PP[:, :, SEQ:]).then_inc(b_stored, 16)
                if 28 <= t <= 29:
                    for b in (0, 1) if t == 28 else (2, 3):
                        act.wait_ge(misc_full, MISC_AT[f"b{b}"] + 1)
                        act.activation(T2[:, b, :], misc_bank(f"b{b}")[:, 0:T], ACT.Copy,
                                       scale=v("pool_scale", b)).then_inc(b_out, 1)
                if t == 29:
                    square(T2, b_out, NG)
                if t == 30:
                    root(NORM["b_rms"])
                if t == 33:
                    mixer_hi(MIX_B, T2)
                if t == 34:
                    square(T0, d_cent, NG, "b_rms")
                if t == 35:
                    root(NORM["d_var"])
                if t == 37:
                    for b in range(NG):
                        act.wait_ge(d_unit, b + 1)
                        act.activation(T0[:, b, :], T0[:, b, :], ACT.Identity, bias=v("sgu_ln_b", b),
                                       scale=v("sgu_ln_g", b)).then_inc(vn_ready, 1)
                if t == 38:
                    for c in range(3):
                        n = P if c < 2 else NB * NS
                        act.wait_ge(misc_full, MISC_AT[f"vt{c}"] + 1)
                        act.activation(vt[0:n, c, :], misc_bank(f"vt{c}")[0:n, :], ACT.Copy).then_inc(vt_ready, 1)
                    act.dma_start(o["v"], T0[:, :, SEQ:]).then_inc(v_stored, 16)
                if t == 42:
                    square(T4, d_out, NG, "d_var")
                if t == 43:
                    root(NORM["d_rms"])
                if t == 45:
                    mixer_hi(MIX_D, T4)
                if t == 56:
                    act.wait_ge(banks_free, use_of(6, NG - 1) + 1)
                    act.dma_start(o["c"], C[:, :, SEQ:]).then_inc(c_stored, 16)
                if t == 57:
                    square(T1, a_cent, NG, "d_rms")
                if t == 58:
                    root(NORM["a_var"])
                if t == 60:
                    act.wait_ge(a_stored, 16)
                    for b in range(NG):
                        act.wait_ge(a_unit, b + 1)
                        act.activation(SG[:, b, :], T1[:, b, :], ACT.Sigmoid, bias=v("ln_a_b", b),
                                       scale=v("ln_a_g", b))
                        act.activation(T1[:, b, :], T1[:, b, :], ACT.Identity, bias=v("ln_a_b", b),
                                       scale=v("ln_a_g", b)).then_inc(a_act, 1)
                if t == 62:
                    square(T1, a_out, NG, "a_var")
                if t == 63:
                    root(NORM["a_rms"])
                if t == 64:
                    square(T2, banks_free, use_of(S_OUT - 1, NG - 1) + 1, "a_rms")
                if t == 65:
                    mixer_hi(MIX_A, T1)
                    root(NORM["c_rms"])
                if t == 67:
                    mixer_hi(MIX_C, T2)
                if T_OUT < t <= T_G0 and t % PER == 0:
                    for b in range((t - T_OUT) // PER * NG - NG, (t - T_OUT) // PER * NG):
                        act.wait_ge(banks_free, use_of(S_OUT + b // NG, b % NG) + 1)
                        act.activation(XH[:, b, :], X[:, b, :], ACT.Copy, scale=v("norm_ffn_g", b)).then_inc(y_hi, 1)
                if t == T_G0 + 4:
                    root(NORM["s2"])
                if t == T_U0:
                    for b in range(NG):
                        act.wait_ge(banks_free, use_of(S_G0, b) + 1)
                        act.activation(T0[:, b, :], SG[:, b, :], ACT.Sigmoid).then_inc(ffn_sig, 1)

            def hidden_hi(count):
                for b in range(NG):
                    act.wait_ge(banks_free, count + b + 1)
                    act.activation(MH[:, b, :], HU[:, b, :], ACT.Copy).then_inc(h_hi, 1)

            hidden_hi(use_of(S_U0, 0))
            with act.Fori(0, NF - 1) as g:
                for j in range(BODY):
                    t = T_LOOP + j + AHEAD
                    hi(t, g * (16 * BODY // RING) + 16 * (t // RING + 1), g * BODY + (t - RING + 1))
                    if j == PER:
                        for b in range(NG):
                            act.wait_ge(banks_free, g * (S_BODY * NG) + (use_of(S_LOOP, b) + 1))
                            act.activation(T0[:, b, :], SG[:, b, :], ACT.Sigmoid).then_inc(ffn_sig, 1)
                    if j == BODY - 1:
                        hidden_hi(g * (S_BODY * NG) + use_of(S_LOOP + S_BODY - 1, 0))
            for t in range(T_END, TILES):
                hi_at(t + AHEAD)
            for n in range(NG):
                act.wait_ge(banks_free, use_of(S_ALL - 1, n) + 1)
                act.activation(SQ[:, n, :], X[:, KD - NG + n, :], ACT.Square).then_inc(last_sq, 1)
            root(NORM["s3"])

        @block.vector
        def _(dve):
            chain = Chain(dve, dve_chain)
            taps_done = [0]

            def lo(t, count):
                dve.wait_ge(hi_ready, count)
                dve.tensor_tensor(slot(wl, t), slot(raw, t), slot(wh, t).bitcast(F32), ALU.subtract).then_inc(lo_ready, 1)

            def lo_at(t):
                if t < TILES:
                    lo(t, t + 1)

            def strip_block(strip, n, last_tile):
                if n < NG - 1:
                    dve.wait_ge(banks_full, full_at(strip, n))
                else:
                    dve.wait_ge(tile_used, last_tile + 1)
                return bank[use_of(strip, n) % BANKS]

            def in_block(strip, n):
                return strip_block(strip, n, (strip + 1) * PER - 1)

            def x_part(b):
                dve.wait_ge(x_hi, b + 1)
                dve.scalar_tensor_tensor(out=XL[:, b, :], in0=X[:, b, :], scalar=v("norm_mix_g", b),
                                         in1=XH[:, b, :].bitcast(F32), op0=ALU.mult, op1=ALU.subtract).then_inc(x_lo, 1)

            def var_out(name, k_set=0):
                dve.wait_ge(misc_full, MISC_AT[name] + 1)
                dve.tensor_scalar(SETS[k_set][0], misc_bank(name)[:, 0:T], EPS, None, ALU.add).then_inc(var_ready, 1)

            def inv_root(k, dst, k_set=0):
                var, r, t = SETS[k_set]
                dve.wait_ge(sd_ready, k + 1)
                chain(dve.reciprocal(r, r))
                chain(dve.tensor_tensor(t, r, r, ALU.mult))
                chain(dve.scalar_tensor_tensor(out=t, in0=t, scalar=-0.5, in1=var, op0=ALU.mult, op1=ALU.mult))
                chain(dve.scalar_tensor_tensor(out=dst, in0=t, scalar=1.5, in1=r, op0=ALU.add, op1=ALU.mult))

            def scale_mixer(m, y, k, k_set=0):
                r = SETS[k_set][1]
                inv_root(k, r, k_set)
                for b in range(NG):
                    dve.scalar_tensor_tensor(out=y[:, b, :], in0=y[:, b, :], scalar=v("out_norm_g", m * NG + b),
                                             in1=r, op0=ALU.mult, op1=ALU.mult).then_inc(scaled[m], 1)

            def mixer_lo(m, y):
                for b in range(NG):
                    dve.wait_ge(mix_hi[m], b + 1)
                    dve.tensor_tensor(ML[:, m * NG + b, :], y[:, b, :], MH[:, m * NG + b, :].bitcast(F32),
                                      ALU.subtract).then_inc(mix_lo[m], 1)

            def conv_taps(n):
                for k in range(taps_done[0], taps_done[0] + n):
                    for b in range(VG):
                        src, acc = G[:, b, k:k + SEQ], T1[:, b, 0:SEQ]
                        if k == 0:
                            ins = dve.tensor_scalar(acc, src, tap(0, b), v("conv_a_b", b), ALU.mult, ALU.add)
                        else:
                            dve.wait_ge(conv_done, (k - 1) * VG + b + 1)
                            ins = dve.scalar_tensor_tensor(out=acc, in0=src, scalar=tap(k, b), in1=acc,
                                                           op0=ALU.mult, op1=ALU.add)
                        ins.then_inc(conv_done, 1)
                taps_done[0] += n

            def short_conv(b):
                for k in range(SW):
                    for h in range(2):
                        src, acc, w = c_at(b, k)[h], two(T2[:, b, :])[h], v("sconv_w", k * NG + b)
                        if k == 0:
                            ins = dve.tensor_scalar(acc, src, w, None, ALU.mult)
                        else:
                            ins = dve.scalar_tensor_tensor(out=acc, in0=src, scalar=w, in1=acc,
                                                           op0=ALU.mult, op1=ALU.add)
                        if h == 1:
                            chain(ins)
                chain(dve.tensor_tensor(T2[:, b, :], T2[:, b, :], s_bc[:, :], ALU.mult))

            def pooling(b):
                w = 2 << b
                src, width = PP[:, b, :], 1
                if b:
                    dve.wait_ge(pooled, b)
                for level in range(b + 1):
                    dst = (S_A, S_B)[level % 2]
                    start = 2 * width - 1
                    chain(dve.tensor_tensor(dst[:, start:PL], src[:, start:PL], src[:, start - width:PL - width], ALU.add))
                    src, width = dst, 2 * width
                assert width == w
                sums_at = (src[:, PW:PA], src[:, PA:PL].rearrange("p (s r) -> p s r", s=NB)[:, :, PW:PS])
                for h in range(2):
                    ins = dve.scalar_tensor_tensor(out=two(T2[:, b, :])[h], in0=sums_at[h], scalar=1.0 / w,
                                                   in1=p_at(b, PW)[h], op0=ALU.mult, op1=ALU.subtract)
                    chain(ins)
                head = sums_at[0][:, 0:w - 1]
                chain(dve.tensor_tensor(head, head, inv[:, 0:w - 1], ALU.mult))
                dve.tensor_tensor(T2[:, b, 0:w - 1], head, PP[:, b, PW:PW + w - 1], ALU.subtract).then_inc(pooled, 1)

            def residual(b, src):
                dve.tensor_tensor(X[:, b, :], src[:, 0:T], X[:, b, :], ALU.add).then_inc(banks_free, 1)

            def hidden_lo(b, count):
                dve.wait_ge(h_hi, count)
                dve.tensor_tensor(ML[:, b, :], HU[:, b, :], MH[:, b, :].bitcast(F32), ALU.subtract).then_inc(h_lo, 1)

            def silu(count):
                for n in range(NG):
                    dve.wait_ge(ffn_sig, count + n + 1)
                    dve.tensor_tensor(SG[:, n, :], SG[:, n, :], T0[:, n, :], ALU.mult).then_inc(ffn_silu, 1)
                for n in range(NG):
                    dve.wait_ge(ffn_silu, count + n + 1)
                    dve.tensor_tensor(SG[:, n, :], SG[:, n, :], s_bc[:, :], ALU.mult).then_inc(ffn_scaled, 1)

            dve.wait_ge(vec_landed, 16)
            for b in range(KD):
                x_part(b)
                if b in (1, 5, 9):
                    lo_at((b - 1) // 4)

            for t in range(T_LOOP):
                lo_at(t + AHEAD)
                if t in TAPS:
                    if t == 16:
                        dve.wait_ge(glu_ready, NG)
                        dve.wait_ge(pads_ready, 4)
                    conv_taps(TAPS[t])
                if t == 6:
                    var_out("s1")
                if t == 7:
                    inv_root(NORM["s1"], s_bc[:, :])
                    chain(dve.tensor_tensor(s2_bc[:, :], s_bc[:, :], s_bc[:, :], ALU.mult))
                    for n in range(NG):
                        src = in_block(0, n)
                        dve.tensor_tensor(T0[:, n, :], src[:, 0:T], s_bc[:, :], ALU.mult).then_inc(banks_free, 1)
                if t == 9:
                    for n in range(NG):
                        dve.wait_ge(gate_sig, n + 1)
                        chain(dve.tensor_tensor(T0[:, n, :], T0[:, n, :], s_bc[:, :], ALU.mult))
                if t == 15:
                    dve.wait_ge(hist_landed, 48)
                    for n in range(NG):
                        src, dst, sig = two(in_block(1, n)[:, 0:T]), g_at(n, CW - 1), two(T0[:, n, :])
                        dve.tensor_tensor(dst[0], src[0], sig[0], ALU.mult).then_inc(glu_ready, 1)
                        dve.tensor_tensor(dst[1], src[1], sig[1], ALU.mult).then_inc(banks_free, 1)
                if t == 23:
                    for n in range(NG):
                        src, dst, s = two(in_block(2, n)[:, 0:T]), p_at(n, PW), two(s_bc[:, :])
                        dve.tensor_tensor(dst[0], src[0], s[0], ALU.mult).then_inc(pin_ready, 1)
                        dve.tensor_tensor(dst[1], src[1], s[1], ALU.mult).then_inc(banks_free, 1)
                if t == 24:
                    dve.wait_ge(banks_free, use_of(2, NG - 1) + 1)
                if 24 <= t <= 27:
                    pooling(t - 24)
                if t == 30:
                    var_out("b_rms")
                if t == 32:
                    scale_mixer(MIX_B, T2, NORM["b_rms"])
                if t == 33:
                    mixer_lo(MIX_B, T2)
                if t == 31:
                    for n in range(NG):
                        src = in_block(3, n)
                        dve.tensor_tensor(T0[:, n, :], src[:, 0:T], s_bc[:, :], ALU.mult).then_inc(banks_free, 1)
                if t == 33:
                    dve.wait_ge(misc_full, MISC_AT["d_mean"] + 1)
                    for n in range(NG):
                        dve.tensor_tensor(T0[:, n, :], T0[:, n, :], misc_bank("d_mean")[:, 0:T],
                                          ALU.subtract).then_inc(d_cent, 1)
                if t == 35:
                    var_out("d_var")
                if t == 36:
                    r = SETS[0][1]
                    inv_root(NORM["d_var"], r)
                    for n in range(NG):
                        dve.tensor_tensor(T0[:, n, :], T0[:, n, :], r, ALU.mult).then_inc(d_unit, 1)
                if t == 39:
                    for n in range(NG):
                        src = in_block(4, n)
                        dve.tensor_tensor(T4[:, n, :], src[:, 0:T], s_bc[:, :], ALU.mult).then_inc(banks_free, 1)
                if 40 <= t <= 41:
                    for n in (0, 1) if t == 40 else (2, 3):
                        dve.wait_ge(banks_free, use_of(4, n) + 1)
                        dve.wait_ge(misc_full, MISC_AT[f"z{n}"] + 1)
                        dve.tensor_tensor(T4[:, n, :], misc_bank(f"z{n}")[:, 0:T], T4[:, n, :],
                                          ALU.mult).then_inc(d_out, 1)
                if t == 43:
                    var_out("d_rms")
                if t == 44:
                    scale_mixer(MIX_D, T4, NORM["d_rms"])
                if t == 45:
                    mixer_lo(MIX_D, T4)
                if t == 47:
                    dve.wait_ge(misc_full, MISC_AT["vt2"] + 1)
                    dve.wait_ge(v_stored, 16)
                    for n in range(NG):
                        src = in_block(5, n)
                        dve.tensor_tensor(T0[:, n, :], src[:, 0:T], s2_bc[:, :], ALU.mult).then_inc(banks_free, 1)
                if t == 55:
                    for n in range(NG):
                        src, dst, ch = two(in_block(6, n)[:, 0:T]), c_at(n, SW - 1), two(T0[:, n, :])
                        dve.tensor_tensor(dst[0], src[0], ch[0], ALU.mult).then_inc(cin_ready, 1)
                        dve.tensor_tensor(dst[1], src[1], ch[1], ALU.mult).then_inc(banks_free, 1)
                if t == 56:
                    dve.wait_ge(misc_full, MISC_AT["a_mean"] + 1)
                    for n in range(NG):
                        dve.tensor_tensor(T1[:, n, :], T1[:, n, :], misc_bank("a_mean")[:, 0:T],
                                          ALU.subtract).then_inc(a_cent, 1)
                    dve.wait_ge(banks_free, use_of(6, NG - 1) + 1)
                if t in (57, 58, 60, 61):
                    short_conv((57, 58, 60, 61).index(t))
                if t == 58:
                    var_out("a_var", 1)
                if t == 59:
                    r = SETS[1][1]
                    inv_root(NORM["a_var"], r, 1)
                    for n in range(NG):
                        dve.tensor_tensor(T1[:, n, :], T1[:, n, :], r, ALU.mult).then_inc(a_unit, 1)
                if t == 61:
                    for n in range(NG):
                        dve.wait_ge(a_act, n + 1)
                        dve.tensor_tensor(T1[:, n, :], T1[:, n, :], SG[:, n, :], ALU.mult).then_inc(a_out, 1)
                if t == 63:
                    var_out("a_rms", 1)
                    for n in range(NG):
                        src = in_block(7, n)
                        dve.tensor_tensor(T2[:, n, :], src[:, 0:T], T2[:, n, :], ALU.mult).then_inc(banks_free, 1)
                if t == 64:
                    scale_mixer(MIX_A, T1, NORM["a_rms"], 1)
                if t == 65:
                    mixer_lo(MIX_A, T1)
                    var_out("c_rms")
                if t == 66:
                    scale_mixer(MIX_C, T2, NORM["c_rms"])
                if t == 67:
                    mixer_lo(MIX_C, T2)
                if T_OUT <= t < T_G0 and t % PER == PER - 1:
                    for n in range(NG):
                        s = (t - T_OUT) // PER
                        residual(s * NG + n, strip_block(S_OUT + s, n, t))
                if T_OUT < t <= T_G0 and t % PER == 0:
                    for b in range((t - T_OUT) // PER * NG - NG, (t - T_OUT) // PER * NG):
                        dve.wait_ge(y_hi, b + 1)
                        dve.scalar_tensor_tensor(out=XL[:, b, :], in0=X[:, b, :], scalar=v("norm_ffn_g", b),
                                                 in1=XH[:, b, :].bitcast(F32), op0=ALU.mult,
                                                 op1=ALU.subtract).then_inc(y_lo, 1)
                if t == T_G0 + 4:
                    var_out("s2")
                if t == T_G0 + 5:
                    inv_root(NORM["s2"], s_bc[:, :])
                if t == T_U0 - 1:
                    for n in range(NG):
                        src = strip_block(S_G0, n, t)
                        dve.tensor_tensor(SG[:, n, :], src[:, 0:T], s_bc[:, :], ALU.mult).then_inc(banks_free, 1)
                if t == T_U0 + 1:
                    silu(0)
                if t == T_LOOP - 1:
                    dve.wait_ge(ffn_scaled, NG)
                    for n in range(NG):
                        src = strip_block(S_U0, n, t)
                        dve.tensor_tensor(HU[:, n, :], src[:, 0:T], SG[:, n, :], ALU.mult).then_inc(banks_free, 1)
                        if n:
                            hidden_lo(n - 1, n)
                    hidden_lo(NG - 1, NG)

            with dve.Fori(0, NF - 1) as g:
                def loop_block(i, n, j):
                    if n < NG - 1:
                        dve.wait_ge(banks_full, g * ((NG - 1) * S_BODY) + full_at(S_LOOP + i, n))
                    else:
                        dve.wait_ge(tile_used, g * BODY + (T_LOOP + j + 1))
                    return bank[use_of(S_LOOP + i, n) % BANKS]

                for j in range(BODY):
                    t = T_LOOP + j + AHEAD
                    lo(t, g * BODY + (t + 1))
                    if j == PER - 1:
                        for n in range(NG):
                            src = loop_block(0, n, j)
                            dve.tensor_tensor(SG[:, n, :], src[:, 0:T], s_bc[:, :], ALU.mult).then_inc(banks_free, 1)
                    if PER < j < BODY - PER and j % PER_DN == PER_DN - 1:
                        s = (j - PER) // PER_DN
                        for n in range(NG):
                            residual(s * NG + n, loop_block(1 + s, n, j))
                    if j == PER + 2:
                        silu(g * NG + NG)
                    if j == BODY - 1:
                        dve.wait_ge(ffn_scaled, g * NG + 2 * NG)
                        for n in range(NG):
                            src = loop_block(S_BODY - 1, n, j)
                            dve.tensor_tensor(HU[:, n, :], src[:, 0:T], SG[:, n, :], ALU.mult).then_inc(banks_free, 1)
                            if n:
                                hidden_lo(n - 1, g * NG + (NG + n))
                        hidden_lo(NG - 1, g * NG + 2 * NG)
            for t in range(T_END, TILES):
                lo_at(t + AHEAD)
                if (t - T_END) % PER_DN == PER_DN - 1:
                    s = (t - T_END) // PER_DN
                    for n in range(NG):
                        residual(s * NG + n, strip_block(S_END + s, n, t))

            var_out("s3")
            inv_root(NORM["s3"], s_bc[:, :])
            dve.wait_ge(dve_chain, chain.n)
            for b in range(KD):
                dve.scalar_tensor_tensor(out=X[:, b, :], in0=X[:, b, :], scalar=v("final_norm_g", b), in1=s_bc[:, :],
                                         op0=ALU.mult, op1=ALU.mult).then_inc(y_ready, 1)

        @block.tensor
        def _(pe):
            def into(name):
                i = MISC_AT[name]
                if i >= 2:
                    s, count = TAKEN[MISC[i - 2]]
                    pe.wait_ge(SEMS[s], count)
                return misc_bank(name)

            def sum_over(name, weights, src):
                M = into(name)
                for b in range(NG):
                    last = pe.matmul(M[:, 0:T], weights[:, :], src[:, b, :], start=(b == 0), stop=(b == NG - 1))
                last.then_inc(misc_full, 1)

            def turn(name, parts):
                for out, in_ in parts:
                    k = in_.shape[0]
                    last = pe.transpose(out, in_, ident[0:k, 0:k])
                last.then_inc(misc_full, 1)

            def products(t, banks, moving, first, last, free_count, moving_ready=None):
                W_H, W_L = (slot(x, t).rearrange("p (k n) -> p k n", k=TK) for x in (wh, wl))
                if moving_ready is not None:
                    pe.wait_ge(*moving_ready)
                for n in range(NG):
                    if first and not (isinstance(free_count, int) and free_count + n <= 0):
                        pe.wait_ge(banks_free, free_count + n)
                    for k in range(TK):
                        hi_, lo_ = moving(k)
                        cols = slice(n * P, (n + 1) * P)
                        pe.matmul(banks[n][:, 0:T], W_H[:, k, cols], hi_, start=(first and k == 0), stop=False)
                        pe.matmul(banks[n][:, 0:T], W_H[:, k, cols], lo_, start=False, stop=False)
                        mm = pe.matmul(banks[n][:, 0:T], W_L[:, k, cols], hi_, start=False, stop=(last and k == TK - 1))
                    if last and n < NG - 1:
                        mm.then_inc(banks_full, 1)
                mm.then_inc(tile_used, 1)

            def strip_banks(strip):
                return [bank[use_of(strip, n) % BANKS] for n in range(NG)]

            def tile(t, strip, kt, tiles, xh, xl, base, moving_ready=None):
                pe.wait_ge(lo_ready, t + 1)
                products(t, strip_banks(strip), lambda k: (xh[:, base + k, :], xl[:, base + k, :]), kt == 0,
                         kt == tiles - 1, use_of(strip, 0) - BANKS + 1, moving_ready)

            for t in range(T_LOOP):
                if t < T_OUT:
                    s, kt = divmod(t, PER)
                    tile(t, s, kt, PER, XH, XL, kt * TK, (x_lo, kt * TK + TK) if s == 0 else None)
                elif t < T_G0:
                    s, kt = divmod(t - T_OUT, PER)
                    m, half = OUT_ORDER[kt // 2], kt % 2
                    tile(t, S_OUT + s, kt, PER, MH, ML, m * NG + half * TK,
                         (mix_lo[m], half * TK + TK) if s == 0 else None)
                else:
                    s, kt = divmod(t - T_G0, PER)
                    tile(t, S_G0 + s, kt, PER, XH, XL, kt * TK, (y_lo, kt * TK + TK) if s == 0 else None)
                if t == 5:
                    M = into("s1")
                    pe.wait_ge(const_ready, 4)
                    pe.wait_ge(sums, 1)
                    pe.matmul(M[:, 0:T], ones_d[:, :], sum_sq[:, :], start=True, stop=True).then_inc(misc_full, 1)
                if 27 <= t <= 28:
                    for b in (0, 1) if t == 27 else (2, 3):
                        M = into(f"b{b}")
                        pe.wait_ge(pooled, b + 1)
                        if b == 0:
                            pe.wait_ge(mats_landed, 32)
                        pe.matmul(M[:, 0:T], PWV[:, b, :], T2[:, b, :], start=True, stop=True).then_inc(misc_full, 1)
                if t == 29:
                    pe.wait_ge(squares, NG)
                    sum_over("b_rms", ones_g, SQ)
                if t == 32:
                    pe.wait_ge(banks_free, use_of(3, NG - 1) + 1)
                    sum_over("d_mean", ones_g, T0)
                if t == 34:
                    pe.wait_ge(squares, 2 * NG)
                    sum_over("d_var", ones_g, SQ)
                if t == 37:
                    pe.wait_ge(vn_ready, NG)
                    for c in range(3):
                        M, n = into(f"vt{c}"), P if c < 2 else NB * NS
                        turn(f"vt{c}", [(M[0:n, b * P:(b + 1) * P], T0[:, b, c * P:c * P + n]) for b in range(NG)])
                if 39 <= t <= 40:
                    pe.wait_ge(vt_ready, 3)
                    pe.wait_ge(masked, 1)
                    pe.wait_ge(corner_landed, 16 * NB)
                    for b in (0, 1) if t == 39 else (2, 3):
                        M, cols = into(f"z{b}"), slice(b * P, (b + 1) * P)
                        for c in range(2):
                            out = M[:, c * P:(c + 1) * P]
                            pe.matmul(out, vt[:, c, cols], WT[:, b, :], start=True, stop=False)
                            pe.matmul(out, ones[0:1, :], BROW[:, b, :], start=False, stop=True)
                        out = M[:, SEQ:T]
                        pe.matmul(out, vt[0:NB * NS, 2, cols], BD[:, b, :], start=True, stop=False)
                        bias = BROW[:, b, 0:NS].unsqueeze(1).to_broadcast([1, NB, NS])
                        pe.matmul(out, ones[0:1, :], bias, start=False, stop=True).then_inc(misc_full, 1)
                if t == 42:
                    pe.wait_ge(squares, 3 * NG)
                    sum_over("d_rms", ones_g, SQ)
                if t == 54:
                    pe.wait_ge(conv_done, CW * VG)
                    pe.wait_ge(conv_s_done, CW)
                    pe.wait_ge(conv_p_done, CW)
                    sum_over("a_mean", ones_g, T1)
                if t == 57:
                    pe.wait_ge(squares, 4 * NG)
                    sum_over("a_var", ones_g, SQ)
                if t == 62:
                    pe.wait_ge(squares, 5 * NG)
                    sum_over("a_rms", ones_g, SQ)
                if t == 64:
                    pe.wait_ge(squares, 6 * NG)
                    sum_over("c_rms", ones_g, SQ)
                if t == T_G0 + 3:
                    M = into("s2")
                    pe.wait_ge(sums, 2)
                    pe.matmul(M[:, 0:T], ones_d[:, :], sum_sq[:, :], start=True, stop=True).then_inc(misc_full, 1)

            with pe.Fori(0, NF - 1) as g:
                for j in range(BODY):
                    t = T_LOOP + j
                    down = PER <= j < BODY - PER
                    if down:
                        i, kt = (j - PER) // PER_DN + 1, (j - PER) % PER_DN
                        tiles, xh, xl, base = PER_DN, MH, ML, kt * TK
                    else:
                        i, kt = (0, j) if j < PER else (S_BODY - 1, j - (BODY - PER))
                        tiles, xh, xl, base = PER, XH, XL, kt * TK
                    pe.wait_ge(lo_ready, g * BODY + (t + 1))
                    products(t, strip_banks(S_LOOP + i), lambda k: (xh[:, base + k, :], xl[:, base + k, :]), kt == 0,
                             kt == tiles - 1, g * (NG * S_BODY) + (use_of(S_LOOP + i, 0) - BANKS + 1),
                             (h_lo, g * NG + NG) if j == PER else None)
            for t in range(T_END, TILES):
                s, kt = divmod(t - T_END, PER_DN)
                tile(t, S_END + s, kt, PER_DN, MH, ML, kt * TK, (h_lo, (NF - 1) * NG + kt * TK + TK) if s == 0 else None)

            M = into("s3")
            pe.wait_ge(sums, 3)
            pe.matmul(M[:, 0:T], ones_d[:, :], sum_sq[:, :], start=True, stop=False)
            for n in range(NG):
                pe.wait_ge(last_sq, n + 1)
                last = pe.matmul(M[:, 0:T], ones_d[:, :], SQ[:, n, :], start=False, stop=(n == NG - 1))
            last.then_inc(misc_full, 1)


def kernel(**inputs):
    import numpy as np
    import concourse.bacc as bacc
    from concourse.bass_utils import run_bass_kernel_spmd

    def rows(name):
        return np.asarray(inputs[name]).reshape(-1, P).T

    def history(name, width, new):
        h = np.asarray(inputs[name])[0].reshape(NB, width, NG, P).transpose(3, 2, 0, 1)
        return np.pad(h, ((0, 0), (0, 0), (0, 0), (0, new))).reshape(P, NG, NB * (width + new))

    tokens = np.concatenate([np.asarray(inputs["x_prompt"])[0], np.asarray(inputs["x_sample"]).reshape(NB * NS, D)])
    host = {
        "x": tokens.reshape(T, KD, P).transpose(2, 1, 0),
        "vec": np.concatenate([rows(name) for name, _ in VECS], axis=1),
        "hist_a": history("state_conv_a", CW - 1, NS),
        "hist_p": history("state_pool", PW, NS),
        "hist_c": history("state_sconv", SW - 1, NS),
        "sgu_wt": np.asarray(inputs["sgu_w"])[0].transpose(2, 0, 1),
    }
    for name in ("w_in", "w_out", "w_gate", "w_up", "w_down", "pool_w", "sgu_b"):
        host[name] = np.asarray(inputs[name])[0]
    shapes = {"y": (P, KD, T), "a": (P, NG, GL - SEQ), "p": (P, NG, PL - SEQ), "c": (P, NG, CL - SEQ),
              "v": (P, NG, NB * NS)}

    nc = bacc.Bacc("TRN2", target_bir_lowering=False, num_devices=1)
    arrays, ins = {}, {}
    for name, x in host.items():
        x = np.ascontiguousarray(x)
        arrays[f"in_{name}"] = x
        ins[name] = nc.dram_tensor(f"in_{name}", x.shape, mybir.dt.from_np(x.dtype), kind="ExternalInput").ap()
    outs = {n: nc.dram_tensor(f"out_{n}", s, F32, kind="ExternalOutput").ap() for n, s in shapes.items()}
    hybrid_step(nc, ins, outs)
    got = run_bass_kernel_spmd(nc, [arrays], core_ids=[0]).results[0]

    y = got["out_y"].transpose(2, 1, 0).reshape(T, D)

    def state(x, kept):
        def last(r):
            r = r[..., -kept:]
            return np.ascontiguousarray(r.transpose(2, 3, 1, 0).reshape(1, -1, kept, GRP))
        return last(x[:, :, None, :kept]), last(x[:, :, kept:].reshape(P, NG, NB, -1))

    new_a, new_p, new_c = (state(got[f"out_{n}"], k) for n, k in (("a", CW - 1), ("p", PW), ("c", SW - 1)))
    chunk_v = got["out_v"].transpose(2, 1, 0).reshape(1, NB, NS, GRP)
    return (np.ascontiguousarray(y[:SEQ]).reshape(1, SEQ, D), np.ascontiguousarray(y[SEQ:]).reshape(NB, NS, D),
            *new_a, *new_p, *new_c, np.ascontiguousarray(chunk_v))
```

```python
from contextlib import ExitStack

import concourse.bass as bass
from concourse import mybir
from concourse.alu_op_type import AluOpType as ALU

ACT = mybir.ActivationFunctionType
F32 = mybir.dt.float32
F32R = mybir.dt.float32r

P = 128
D = 2048
KD = D // P
SEQ = 256
NB, NS = 8, 4
T = SEQ + NB * NS
GRP = 512
NG = GRP // P
F = 5632
NF = F // GRP
CW = 31
PW = 15
SW = 3
EPS = 1e-6

TK = 2
TILE = TK * GRP
RING = 4
BANKS = 6
XQ = 8
AHEAD = RING - 1

GA, GS = CW - 1 + SEQ, CW - 1 + NS
PA, PS = PW + SEQ, PW + NS
CA, CS = SW - 1 + SEQ, SW - 1 + NS
GL, PL, CL = GA + NB * GS, PA + NB * PS, CA + NB * CS

A_VAL, A_GATE, POOL, C_H, C_B, C_C, D_U, D_V = range(8)
STRIPS = [A_GATE, A_VAL, POOL, D_V, D_U, C_H, C_C, C_B]
MIX_A, MIX_B, MIX_C, MIX_D = range(4)
OUT_ORDER = [MIX_B, MIX_D, MIX_A, MIX_C]

PER = D // (TK * P)
T_IN = 0
T_OUT = T_IN + len(STRIPS) * PER
T_G0 = T_OUT + (D // GRP) * PER
T_U0 = T_G0 + PER
T_LOOP = T_U0 + PER
PER_DN = GRP // (TK * P)
BODY = 2 * PER + (D // GRP) * PER_DN
T_END = T_LOOP + (NF - 1) * BODY
TILES = T_END + (D // GRP) * PER_DN

S_OUT = len(STRIPS)
S_G0 = S_OUT + D // GRP
S_U0 = S_G0 + 1
S_LOOP = S_U0 + 1
S_BODY = 2 + D // GRP
S_END = S_LOOP + (NF - 1) * S_BODY
S_ALL = S_END + D // GRP
assert XQ == PER
assert S_BODY * NG % BANKS == 0 and BODY % RING == 0

VECS = [("norm_mix_g", KD), ("conv_a_b", NG), ("ln_a_g", NG), ("ln_a_b", NG), ("pool_scale", NG),
        ("sgu_ln_g", NG), ("sgu_ln_b", NG), ("out_norm_g", KD), ("norm_ffn_g", KD), ("final_norm_g", KD),
        ("sconv_w", SW * NG), ("conv_a_w", CW * NG)]
VROW, NV = {}, 0
for _name, _rows in VECS:
    VROW[_name] = NV
    NV += _rows

NORM = {n: i for i, n in enumerate(["s1", "b_rms", "d_var", "d_rms", "a_var", "a_rms", "c_rms", "s2", "s3"])}
TAKEN = {n: ("var_ready", i + 1) for n, i in NORM.items()}
TAKEN.update({"d_mean": ("d_cent", NG), "a_mean": ("a_cent", NG)})
TAKEN.update({f"b{n}": ("b_out", n + 1) for n in range(NG)})
TAKEN.update({f"vt{n}": ("vt_ready", n + 1) for n in range(3)})
TAKEN.update({f"z{n}": ("d_out", n + 1) for n in range(NG)})
MISC = ["s1", "b0", "b1", "b2", "b3", "b_rms", "d_mean", "d_var", "vt0", "vt1", "vt2", "z0", "z1", "z2", "z3",
        "a_mean", "d_rms", "a_var", "a_rms", "c_rms", "s2", "s3"]
MISC_AT = {name: i for i, name in enumerate(MISC)}

TAPS = {16: 2, 17: 2, 18: 2, 19: 2, 20: 2, 21: 2, 22: 2, 28: 2, 29: 2, 30: 2, 33: 1, 37: 1, 40: 2,
        42: 1, 43: 2, 44: 2, 45: 1, 46: 1}
YP = (2 * NG, NG)
HANDED = 4
WARM = 10
FOLDED = (1, 2)
PARTS = (slice(0, 144), slice(144, T))
CG = 2
VG = NG - 2
assert sum(TAPS.values()) == CW


DR, AM = 50, 49
VAR_AT = {6: "s1", 35: "b_rms", 38: "d_var", DR + 1: "d_rms", AM + 4: "a_var", AM + 11: "a_rms", 66: "c_rms",
          T_G0 + 4: "s2"}
IN_PAIR = ("b_rms", "a_var", "a_rms")


def full_at(strip, n):
    return (NG - 1) * strip + n + 1


def use_of(strip, n):
    return NG * strip + n


def hybrid_step(nc, a, o):
    ctx = ExitStack()
    with ctx:
        def sb(name, cols, dt=F32):
            return ctx.enter_context(nc.sbuf_tensor(name, [P, cols], dt))

        def sem(name):
            return ctx.enter_context(nc.semaphore(name))

        def blocks(t, n=NG):
            return t.rearrange("p (n t) -> p n t", n=n)

        x_sb = sb("x_sb", KD * T)
        xh_sb, xl_sb = sb("xh_sb", KD * T, F32R), sb("xl_sb", KD * T, F32R)
        mh_sb, ml_sb = sb("mh_sb", KD * T, F32R), sb("ml_sb", KD * T, F32R)
        raw = sb("raw", RING * TILE)
        wh, wl = sb("wh", RING * TILE, F32R), sb("wl", RING * TILE, F32R)
        X = blocks(x_sb[:, :], KD)
        XH, XL = blocks(xh_sb[:, :], KD), blocks(xl_sb[:, :], KD)
        MH, ML = blocks(mh_sb[:, :], KD), blocks(ml_sb[:, :], KD)

        NT = NG * T
        T0, T1, T2, T4 = (blocks(sb(f"work{i}", NT)[:, :]) for i in range(4))
        vt = sb("vt", 3 * GRP)[:, :].rearrange("p (c d) -> p c d", c=3)
        g_sb, p_sb, c_sb = sb("g_sb", NG * GL), sb("p_sb", NG * PL), sb("c_sb", NG * CL)
        G, PP, C = blocks(g_sb[:, :]), blocks(p_sb[:, :]), blocks(c_sb[:, :])
        SG = blocks(g_sb[:, 0:NT])
        HU = blocks(p_sb[:, 0:NT])
        sq_sb = sb("sq_sb", NT)
        SQ = blocks(sq_sb[:, :])
        pair = sb("pair", 3 * T)
        B_SUM = blocks(pair[:, 0:2 * T], 2)
        S_A, S_B = pair[:, 0:PL], pair[:, PL:2 * PL]
        norm0 = sb("norm0", 3 * T)
        SETS = [[t[:, i * T:(i + 1) * T] for i in range(3)] for t in (norm0, pair)]
        s_bc = sb("s_bc", T)
        s2_bc = sb("s2_bc", T)
        sum_sq, one_sq = sb("sum_sq", T), sb("one_sq", T)
        prod, prod_s = one_sq[:, 0:SEQ], sum_sq[:, 0:NG * NB * NS]

        ident, ones, ones_d, ones_g = (sb(n, P) for n in ("ident", "ones", "ones_d", "ones_g"))
        vec = sb("vec", NV)
        wt = sb("wt", NG * P)
        bd = sb("bd", NG * NB * NS)
        pw = sb("pw", NG * P)
        brow = sb("brow", NG * P)
        inv = sb("inv", PW)
        scrap = sb("scrap", 1)
        WT, BD = blocks(wt[:, :]), blocks(bd[0:NB * NS, :])
        PWV, BROW = blocks(pw[:, :]), blocks(brow[0:1, :])

        def v(name, b):
            return vec[:, VROW[name] + b:VROW[name] + b + 1]

        def tap(k, b):
            return v("conv_a_w", k * NG + b)

        def halves(buf, b, width, first, at, n):
            prompt = buf[:, b, at:at + first]
            sample = buf[:, b, width:].rearrange("p (s r) -> p s r", s=NB)[:, :, at:at + n]
            return prompt, sample

        def g_at(b, k):
            return halves(G, b, GA, SEQ, k, NS)

        def p_at(b, k):
            return halves(PP, b, PA, SEQ, k, NS)

        def c_at(b, k):
            return halves(C, b, CA, SEQ, k, NS)

        def two(t):
            return t[:, 0:SEQ], t[:, SEQ:T].rearrange("p (s r) -> p s r", s=NB)

        def square_of(b):
            return (T1, T2, T4, SQ)[b // NG][:, b % NG, :]

        def last_square(b):
            return (T0, HU, SG, SQ)[b // NG][:, b % NG, :]

        def gained(b):
            return (T1, T2, T4, T0)[b // NG][:, b % NG, :]

        bank = [ctx.enter_context(nc.psum_tensor(f"bank{i}", [P, 512], F32)) for i in range(BANKS + 2)]

        raw_landed = [sem(f"raw_landed{i}") for i in range(RING)]
        x_landed = [sem(f"x_landed{i}") for i in range(XQ)]
        vec_landed, sgu_landed, mats_landed, hist_landed, corner_landed = (sem(n) for n in (
            "vec_landed", "sgu_landed", "mats_landed", "hist_landed", "corner_landed"))
        first_landed, first_hi, first_lo = (sem(n) for n in ("first_landed", "first_hi", "first_lo"))
        hi_ready, lo_ready, tile_used = sem("hi_ready"), sem("lo_ready"), sem("tile_used")
        banks_full, banks_free = sem("banks_full"), sem("banks_free")
        misc_full, b_out, vt_ready = sem("misc_full"), sem("b_out"), sem("vt_ready")
        x_hi, x_lo, y_hi, y_lo = sem("x_hi"), sem("x_lo"), sem("y_hi"), sem("y_lo")
        const_ready, pads_ready, bd_zero, masked = (sem(n) for n in ("const_ready", "pads_ready", "bd_zero", "masked"))
        sums, pool_chain, dve_chain, act_chain = (sem(n) for n in ("sums", "pool_chain", "dve_chain", "act_chain"))
        var_ready, sd_ready, r_ready = sem("var_ready"), sem("sd_ready"), sem("r_ready")
        gate_sig, glu_ready, conv_done = sem("gate_sig"), sem("glu_ready"), sem("conv_done")
        pin_ready, cin_ready, pooled = sem("pin_ready"), sem("cin_ready"), sem("pooled")
        d_cent, d_unit, vn_ready, d_out = sem("d_cent"), sem("d_unit"), sem("vn_ready"), sem("d_out")
        a_cent, a_unit, a_act, a_out = sem("a_cent"), sem("a_unit"), sem("a_act"), sem("a_out")
        squares, x_squares = sem("squares"), sem("x_squares")
        d_rms_ready, a_rms_ready, sums_dve, x_folded = (sem(n) for n in (
            "d_rms_ready", "a_rms_ready", "sums_dve", "x_folded"))
        halved, quartered = sem("halved"), sem("quartered")
        block_sum, short_done = sem("block_sum"), sem("short_done")
        scaled = [sem(f"scaled{m}") for m in range(4)]
        mix_hi, mix_lo = [sem(f"mix_hi{m}") for m in range(4)], [sem(f"mix_lo{m}") for m in range(4)]
        conv_s_prod, conv_s_done, conv_p_prod, conv_p_done = (sem(n) for n in (
            "conv_s_prod", "conv_s_done", "conv_p_prod", "conv_p_done"))
        ffn_silu, ffn_scaled = sem("ffn_silu"), sem("ffn_scaled")
        ffn_sig, h_hi, h_lo = sem("ffn_sig"), sem("h_hi"), sem("h_lo")
        a_stored, b_stored, v_stored, c_stored = (sem(n) for n in ("a_stored", "b_stored", "v_stored", "c_stored"))
        last_sq, y_ready, y_stored = sem("last_sq"), sem("y_ready"), sem("y_stored")
        y_gained, s_final, y_pool = sem("y_gained"), sem("s_final"), sem("y_pool")
        SEMS = {"b_out": b_out, "vt_ready": vt_ready, "var_ready": var_ready, "d_cent": d_cent, "a_cent": a_cent, "d_out": d_out}

        def w_rows(w, row, col):
            return w[row:row + TK * P, col:col + GRP].rearrange("(k p) n -> p k n", k=TK)

        def tile_source(t):
            if t < T_OUT:
                s, kt = divmod(t, PER)
                return w_rows(a["w_in"], kt * TK * P, STRIPS[s] * GRP)
            if t < T_G0:
                s, kt = divmod(t - T_OUT, PER)
                m, half = OUT_ORDER[kt // 2], kt % 2
                return w_rows(a["w_out"], m * GRP + half * TK * P, s * GRP)
            if t < T_U0:
                return w_rows(a["w_gate"], (t - T_G0) * TK * P, 0)
            if t < T_LOOP:
                return w_rows(a["w_up"], (t - T_U0) * TK * P, 0)
            s, kt = divmod(t - T_END, PER_DN)
            return w_rows(a["w_down"], (NF - 1) * GRP + kt * TK * P, s * GRP)

        def loop_source(g, j):
            if j < PER or j >= BODY - PER:
                w, kt = (a["w_gate"], j) if j < PER else (a["w_up"], j - (BODY - PER))
                return w[kt * TK * P:(kt + 1) * TK * P, bass.ds(g * GRP + GRP, GRP)].rearrange("(k p) n -> p k n", k=TK)
            s, kt = divmod(j - PER, PER_DN)
            return w_down_rows(g, kt)[:, :, s * GRP:(s + 1) * GRP]

        def w_down_rows(g, kt):
            return a["w_down"][bass.ds(g * GRP + kt * TK * P, TK * P), :].rearrange("(k p) n -> p k n", k=TK)

        def slot(buf, t):
            return buf[:, (t % RING) * TILE:(t % RING + 1) * TILE]

        class Chain:
            def __init__(self, eng, s):
                self.eng, self.s, self.n = eng, s, 0

            def __call__(self, ins):
                self.n += 1
                ins.then_inc(self.s, 1)
                self.eng.wait_ge(self.s, self.n)

        def misc_bank(name):
            return bank[BANKS + MISC_AT[name] % 2]

        block = ctx.enter_context(nc.Block())

        @block.sync
        def _(sp):
            def load(t, src, lo_count, landed_in):
                if lo_count is not None:
                    sp.wait_ge(lo_ready, lo_count)
                sp.dma_start(slot(raw, t).rearrange("p (k n) -> p k n", k=TK), src).then_inc(raw_landed[landed_in], 16)

            for t in range(T_LOOP):
                if t < XQ:
                    bs = slice(t * TK, (t + 1) * TK)
                    sp.dma_start(X[:, bs, :], a["x"][:, bs, :]).then_inc(x_landed[t], 16)
                if t == 0:
                    for k, landed in ((0, first_landed), (1, raw_landed[0])):
                        sp.dma_start(raw[:, k * GRP:(k + 1) * GRP], tile_source(0)[:, k, :]).then_inc(landed, 16)
                else:
                    load(t, tile_source(t), t - RING + 1 if t >= RING else None, t % RING)
                if t == XQ:
                    sp.dma_start(WT, a["sgu_wt"]).then_inc(sgu_landed, 16)
                    for buf, width, name in ((G, GA, "hist_a"), (PP, PA, "hist_p"), (C, CA, "hist_c")):
                        sp.dma_start(buf[:, :, width:], a[name]).then_inc(hist_landed, 16)
                    sp.dma_start(PWV, a["pool_w"].rearrange("g c d -> c g d")).then_inc(mats_landed, 16)
                    sp.dma_start(brow[0:1, :], a["sgu_b"].rearrange("(u g) i -> u (g i)", u=1)).then_inc(mats_landed, 16)
            with sp.Fori(0, NF - 1) as g:
                for j in range(BODY):
                    t = T_LOOP + j
                    load(t, loop_source(g, j), g * BODY + (t - RING + 1), t % RING)
            for t in range(T_END, TILES):
                load(t, tile_source(t), t - RING + 1, t % RING)

            for i, h in enumerate(PARTS):
                for m in range(YP[i] // NG, KD // NG):
                    sp.wait_ge(y_ready, i * (KD - YP[0]) // NG + m - YP[i] // NG + 1)
                    bs = slice(m * NG, (m + 1) * NG)
                    sp.dma_start(o["y"][:, bs, h], X[:, bs, h]).then_inc(y_stored, 16)
                for m in range(YP[i] // NG):
                    sp.wait_ge(y_pool, i * YP[0] + m * NG + NG)
                    bs = slice(m * NG, (m + 1) * NG)
                    sp.dma_start(o["y"][:, bs, h], X[:, bs, h]).then_inc(y_stored, 16)
            sp.wait_ge(y_stored, 16 * len(PARTS) * (KD // NG))
            sp.wait_ge(a_stored, 16)
            sp.wait_ge(b_stored, 16)
            sp.wait_ge(v_stored, 16)
            sp.wait_ge(c_stored, 16)

        @block.gpsimd
        def _(pool):
            chain = Chain(pool, pool_chain)
            chain(pool.memset(ident[:, :], 0.0))
            pool.affine_select(out=ident[:, :], in_=ident[:, :], compare_op=ALU.not_equal, fill=1.0, base=0,
                               pattern=[[-1, P]], channel_multiplier=1).then_inc(const_ready, 1)
            pool.memset(ones[:, :], 1.0).then_inc(const_ready, 1)
            pool.memset(ones_d[:, :], 1.0 / D).then_inc(const_ready, 1)
            pool.memset(ones_g[:, :], 1.0 / GRP).then_inc(const_ready, 1)
            pool.memset(bd[0:NB * NS, :], 0.0).then_inc(bd_zero, 1)
            pool.memset(G[:, :, 0:CW - 1], 0.0).then_inc(pads_ready, 1)
            pool.memset(PP[:, :, 0:PW], 0.0).then_inc(pads_ready, 1)
            pool.memset(C[:, :, 0:SW - 1], 0.0).then_inc(pads_ready, 1)
            for t in range(PW):
                last = pool.memset(inv[:, t:t + 1], 1.0 / (t + 1))
            last.then_inc(pads_ready, 1)

            def sum_squares(b, last):
                if b == 0:
                    chain(pool.tensor_tensor(sum_sq[:, :], X[:, b, :], X[:, b, :], ALU.mult))
                    return
                chain(pool.tensor_tensor(one_sq[:, :], X[:, b, :], X[:, b, :], ALU.mult))
                ins = pool.tensor_tensor(sum_sq[:, :], sum_sq[:, :], one_sq[:, :], ALU.add)
                if b == last:
                    ins.then_inc(sums, 1)
                else:
                    chain(ins)

            for b in range(1, KD):
                if b >= KD - 2 or b // NG in FOLDED and b % NG >= 2:
                    continue
                pool.wait_ge(*((x_folded, FOLDED.index(b // NG) + 1) if b // NG in FOLDED else (x_squares, b + 1)))
                ins = pool.tensor_tensor(sum_sq[:, :], square_of(0) if b == 1 else sum_sq[:, :], square_of(b), ALU.add)
                if b == KD - 3:
                    ins.then_inc(sums, 1)
                else:
                    chain(ins)

            pool.wait_ge(sgu_landed, 16)
            pool.affine_select(out=WT, in_=WT, compare_op=ALU.is_ge, fill=0.0, base=0,
                               pattern=[[0, NG], [1, P]], channel_multiplier=-1).then_inc(masked, 1)

            gs = G[:, :, GA:].rearrange("p b (s r) -> p b s r", s=NB)
            ys = T1[:, :, SEQ:].rearrange("p b (s r) -> p b s r", s=NB)
            ps = prod_s.rearrange("p (b s r) -> p b s r", b=NG, s=NB)
            pool.wait_ge(misc_full, MISC_AT["s1"] + 1)
            pool.wait_ge(vec_landed, 16)
            pool.wait_ge(banks_free, use_of(1, NG - 1) + 1)
            pool.wait_ge(hist_landed, 48)
            for b in range(NG):
                pool.tensor_scalar(ys[:, b], gs[:, b, :, 0:NS], tap(0, b), v("conv_a_b", b), ALU.mult,
                                   ALU.add).then_inc(conv_s_done, 1)
            for i, b in enumerate(range(NG - 1, VG - 1, -1)):
                acc = T1[:, b, 0:SEQ]
                for k in range(CW - (HANDED if b == VG else 0)):
                    src, at = G[:, b, k:k + SEQ], i * CW + k
                    if k == 0:
                        pool.tensor_scalar(acc, src, tap(0, b), v("conv_a_b", b), ALU.mult, ALU.add).then_inc(conv_p_done, 1)
                        continue
                    with_samples = i == 0
                    pool.wait_ge(conv_p_done, at - 1 if k == 1 and i else at)
                    if with_samples:
                        w = vec[:, VROW["conv_a_w"] + k * NG:VROW["conv_a_w"] + (k + 1) * NG]
                        w = w.unsqueeze(2).unsqueeze(3).to_broadcast([P, NG, NB, NS])
                        pool.wait_ge(conv_s_done, NG - 1 + k)
                        pool.tensor_tensor(ps, gs[:, :, :, k:k + NS], w, ALU.mult).then_inc(conv_s_prod, 1)
                    pool.tensor_tensor(prod, src, tap(k, b).to_broadcast([P, SEQ]), ALU.mult).then_inc(conv_p_prod, 1)
                    if with_samples:
                        pool.wait_ge(conv_s_prod, k)
                        pool.tensor_tensor(ys, ys, ps, ALU.add).then_inc(conv_s_done, 1)
                    pool.wait_ge(conv_p_prod, at - i)
                    pool.wait_ge(conv_p_done, at)
                    pool.tensor_tensor(acc, acc, prod, ALU.add).then_inc(conv_p_done, 1)

            def block_sums(before, prior):
                pool.wait_ge(squares, before + 2)
                pool.wait_ge(misc_full, MISC_AT[prior] + 1)
                chain(pool.tensor_tensor(one_sq[:, :], SQ[:, 0, :], SQ[:, 1, :], ALU.add))
                for b in range(2, NG):
                    pool.wait_ge(squares, before + b + 1)
                    ins = pool.tensor_tensor(one_sq[:, :], one_sq[:, :], SQ[:, b, :], ALU.add)
                    if b == NG - 1:
                        ins.then_inc(block_sum, 1)
                    else:
                        chain(ins)

            def scale(m, y, r):
                for b in range(NG):
                    g = v("out_norm_g", m * NG + b).to_broadcast([P, T])
                    chain(pool.tensor_tensor(y[:, b, :], y[:, b, :], r, ALU.mult))
                    pool.tensor_tensor(y[:, b, :], y[:, b, :], g, ALU.mult).then_inc(scaled[m], 1)

            pool.wait_ge(conv_p_done, (NG - VG) * CW - HANDED)
            block_sums(2 * NG, "s1")
            block_sums(3 * NG, "d_rms")
            pool.wait_ge(d_rms_ready, 1)
            scale(MIX_D, T4, SETS[0][1])
            for b in range(NG):
                pool.wait_ge(mix_hi[MIX_D], b + 1)
                pool.tensor_tensor(ML[:, MIX_D * NG + b, :], T4[:, b, :], MH[:, MIX_D * NG + b, :].bitcast(F32),
                                   ALU.subtract).then_inc(mix_lo[MIX_D], 1)

            pool.wait_ge(banks_free, use_of(6, NG - 1) + 1)
            for b in range(NG - CG, NG):
                for k in range(SW):
                    for h in range(2):
                        src, acc, w = c_at(b, k)[h], two(T2[:, b, :])[h], v("sconv_w", k * NG + b)
                        if k == 0:
                            ins = pool.tensor_scalar(acc, src, w, None, ALU.mult)
                        else:
                            tmp = two(sum_sq[:, :])[h]
                            wb = w.to_broadcast([P, SEQ]) if h == 0 else w.unsqueeze(2).to_broadcast([P, NB, NS])
                            chain(pool.tensor_tensor(tmp, src, wb, ALU.mult))
                            ins = pool.tensor_tensor(acc, acc, tmp, ALU.add)
                        if h == 1:
                            chain(ins)
                pool.tensor_tensor(T2[:, b, :], T2[:, b, :], s_bc[:, :], ALU.mult).then_inc(short_done, 1)
                if b == NG - CG:
                    block_sums(4 * NG, "a_var")
            pool.wait_ge(a_rms_ready, 1)
            scale(MIX_A, T1, SETS[1][1])
            block_sums(5 * NG, "a_rms")

            for b in range(KD):
                pool.wait_ge(banks_free, use_of(S_OUT + b // NG, b % NG) + 1)
                sum_squares(b, KD - 1)
            pool.wait_ge(misc_full, MISC_AT["s2"] + 1)
            for b in range(1, KD - NG):
                pool.wait_ge(last_sq, b + 1)
                ins = pool.tensor_tensor(sum_sq[:, :], last_square(0) if b == 1 else sum_sq[:, :], last_square(b), ALU.add)
                if b == KD - NG - 1:
                    ins.then_inc(sums, 1)
                else:
                    chain(ins)
            pool.wait_ge(y_gained, KD)
            for i, h in enumerate(PARTS):
                pool.wait_ge(s_final, i + 1)
                for b in range(YP[i]):
                    pool.tensor_tensor(X[:, b, h], gained(b)[:, h], s_bc[:, h], ALU.mult).then_inc(y_pool, 1)

        @block.scalar
        def _(act):
            chain = Chain(act, act_chain)
            act.dma_start(vec[:, :], a["vec"]).then_inc(vec_landed, 16)

            def hi(t, landed, used):
                act.wait_ge(raw_landed[t % RING], landed)
                if used is not None:
                    act.wait_ge(tile_used, used)
                act.activation(slot(wh, t), slot(raw, t), ACT.Copy).then_inc(hi_ready, 1)

            def hi_at(t):
                if t < TILES:
                    hi(t, 16 * (t // RING + 1), t - RING + 1 if t >= RING else None)

            def square(src, ready, count, prior=None):
                act.wait_ge(ready, count)
                if prior is not None:
                    act.wait_ge(misc_full, MISC_AT[prior] + 1)
                for b in range(NG):
                    act.activation(SQ[:, b, :], src[:, b, :], ACT.Square).then_inc(squares, 1)

            def root(k):
                act.wait_ge(var_ready, k + 1)
                s = SETS[k in [NORM[name] for name in IN_PAIR]]
                act.activation(s[1], s[0], ACT.Sqrt).then_inc(sd_ready, 1)

            def mixer_hi(m, src):
                for b in range(NG):
                    act.wait_ge(scaled[m], b + 1)
                    act.activation(MH[:, m * NG + b, :], src[:, b, :], ACT.Copy).then_inc(mix_hi[m], 1)

            def table(func):
                act.activation(scrap[:, :], ones[:, 0:1], func)

            act.wait_ge(const_ready, 2)
            table(ACT.Copy)
            act.wait_ge(vec_landed, 16)
            def x_part(q):
                act.wait_ge(x_landed[q], 16)
                for b in range(q * TK, (q + 1) * TK):
                    act.activation(XH[:, b, :], X[:, b, :], ACT.Copy, scale=v("norm_mix_g", b)).then_inc(x_hi, 1)

            x_part(0)
            act.wait_ge(first_landed, 16)
            act.activation(wh[:, 0:GRP], raw[:, 0:GRP], ACT.Copy).then_inc(first_hi, 1)
            act.wait_ge(raw_landed[0], 16)
            act.activation(wh[:, GRP:TILE], raw[:, GRP:TILE], ACT.Copy).then_inc(hi_ready, 1)
            for q in range(1, AHEAD):
                x_part(q)
                hi_at(q)

            for t in range(T_LOOP):
                if t + AHEAD < XQ:
                    x_part(t + AHEAD)
                if t == 6:
                    root(NORM["s1"])
                if t != 4:
                    hi_at(t + AHEAD)
                for b in range(min(NG * t, TK * (t + AHEAD)), min(NG * t + NG, TK * (t + AHEAD + 1), KD)):
                    act.activation(square_of(b), X[:, b, :], ACT.Square).then_inc(x_squares, 1)
                if t == 4:
                    hi_at(t + AHEAD)
                if t == 5:
                    table(ACT.Sqrt)
                if t in VAR_AT and t != 6:
                    root(NORM[VAR_AT[t]])
                if t == 8:
                    for b in range(NG):
                        act.wait_ge(banks_free, use_of(0, b) + 1)
                        act.activation(T0[:, b, :], T0[:, b, :], ACT.Sigmoid).then_inc(gate_sig, 1)
                if t == 12:
                    act.wait_ge(masked, 1)
                    act.wait_ge(bd_zero, 1)
                    for s in range(NB):
                        act.dma_start(BD[s * NS:(s + 1) * NS, :, s * NS:(s + 1) * NS],
                                      WT[0:NS, :, 0:NS]).then_inc(corner_landed, 16)
                if t == 17:
                    act.wait_ge(banks_free, use_of(1, NG - 1) + 1)
                    act.wait_ge(hist_landed, 48)
                    act.dma_start(o["a"], G[:, :, SEQ:]).then_inc(a_stored, 16)
                if t == 24:
                    act.wait_ge(banks_free, use_of(2, NG - 1) + 1)
                    act.dma_start(o["p"], PP[:, :, SEQ:]).then_inc(b_stored, 16)
                if 29 <= t <= 30:
                    for b in (0, 1) if t == 29 else (2, 3):
                        act.wait_ge(misc_full, MISC_AT[f"b{b}"] + 1)
                        act.activation(T2[:, b, :], misc_bank(f"b{b}")[:, 0:T], ACT.Copy,
                                       scale=v("pool_scale", b)).then_inc(b_out, 1)
                if t == 31:
                    square(T2, b_out, NG)
                if t == 43:
                    mixer_hi(MIX_B, T2)
                if t == 35:
                    square(T0, d_cent, NG, "b_rms")
                if t == 40:
                    for b in range(NG):
                        act.wait_ge(d_unit, b + 1)
                        act.activation(T0[:, b, :], T0[:, b, :], ACT.Identity, bias=v("sgu_ln_b", b),
                                       scale=v("sgu_ln_g", b)).then_inc(vn_ready, 1)
                if 42 <= t <= 43:
                    for c in (0, 1) if t == 42 else (2,):
                        n = P if c < 2 else NB * NS
                        act.wait_ge(misc_full, MISC_AT[f"vt{c}"] + 1)
                        act.activation(vt[0:n, c, :], misc_bank(f"vt{c}")[0:n, :], ACT.Copy).then_inc(vt_ready, 1)
                if t == 43:
                    act.dma_start(o["v"], T0[:, :, SEQ:]).then_inc(v_stored, 16)
                if t == 48:
                    square(T4, d_out, NG, "d_var")
                if t == DR + 4:
                    mixer_hi(MIX_D, T4)
                if t == 56:
                    act.wait_ge(banks_free, use_of(6, NG - 1) + 1)
                    act.dma_start(o["c"], C[:, :, SEQ:]).then_inc(c_stored, 16)
                if t == AM + 2:
                    act.wait_ge(block_sum, 1)
                    square(T1, a_cent, NG)
                if t == AM + 6:
                    act.wait_ge(a_stored, 16)
                    for b in range(NG):
                        act.wait_ge(a_unit, b + 1)
                        act.activation(SG[:, b, :], T1[:, b, :], ACT.Sigmoid, bias=v("ln_a_b", b),
                                       scale=v("ln_a_g", b))
                        act.activation(T1[:, b, :], T1[:, b, :], ACT.Identity, bias=v("ln_a_b", b),
                                       scale=v("ln_a_g", b)).then_inc(a_act, 1)
                if t == AM + 8:
                    square(T1, a_out, NG, "a_var")
                if t == 64:
                    square(T2, banks_free, use_of(S_OUT - 1, NG - 1) + 1, "a_rms")
                if t == 65:
                    mixer_hi(MIX_A, T1)
                if t == 67:
                    mixer_hi(MIX_C, T2)
                if T_OUT < t <= T_G0 and t % PER == 0:
                    for b in range((t - T_OUT) // PER * NG - NG, (t - T_OUT) // PER * NG):
                        act.wait_ge(banks_free, use_of(S_OUT + b // NG, b % NG) + 1)
                        act.activation(XH[:, b, :], X[:, b, :], ACT.Copy, scale=v("norm_ffn_g", b)).then_inc(y_hi, 1)
                if t == T_U0:
                    for b in range(NG):
                        act.wait_ge(banks_free, use_of(S_G0, b) + 1)
                        act.activation(T0[:, b, :], SG[:, b, :], ACT.Sigmoid).then_inc(ffn_sig, 1)

            def hidden_hi(count):
                for b in range(NG):
                    act.wait_ge(banks_free, count + b + 1)
                    act.activation(MH[:, b, :], HU[:, b, :], ACT.Copy).then_inc(h_hi, 1)

            hidden_hi(use_of(S_U0, 0))
            with act.Fori(0, NF - 1) as g:
                for j in range(BODY):
                    t = T_LOOP + j + AHEAD
                    hi(t, g * (16 * BODY // RING) + 16 * (t // RING + 1), g * BODY + (t - RING + 1))
                    if j == PER:
                        for b in range(NG):
                            act.wait_ge(banks_free, g * (S_BODY * NG) + (use_of(S_LOOP, b) + 1))
                            act.activation(T0[:, b, :], SG[:, b, :], ACT.Sigmoid).then_inc(ffn_sig, 1)
                    if j == BODY - 1:
                        hidden_hi(g * (S_BODY * NG) + use_of(S_LOOP + S_BODY - 1, 0))

            def last_squares(m):
                for b in range(m * NG, m * NG + NG):
                    act.wait_ge(banks_free, use_of(S_END, b) + 1)
                    act.activation(last_square(b), X[:, b, :], ACT.Square).then_inc(last_sq, 1)

            def gain(m):
                for b in range(m * NG, m * NG + NG):
                    act.activation(gained(b), X[:, b, :], ACT.Copy, scale=v("final_norm_g", b)).then_inc(y_gained, 1)

            table(ACT.Sqrt)
            for t in range(T_END, TILES):
                hi_at(t + AHEAD)
                if t > T_END and (t - T_END) % PER_DN == 0:
                    last_squares((t - T_END) // PER_DN - 1)
                    gain((t - T_END) // PER_DN - 1)
            last_squares(KD // NG - 1)
            for i, h in enumerate(PARTS):
                act.wait_ge(var_ready, len(NORM) + i)
                act.activation(SETS[0][1][:, h], SETS[0][0][:, h], ACT.Sqrt).then_inc(sd_ready, 1)
            act.wait_ge(sums, 3)
            gain(KD // NG - 1)

        @block.vector
        def _(dve):
            chain = Chain(dve, dve_chain)
            taps_done = [0]

            def lo(t, count):
                dve.wait_ge(hi_ready, count)
                dve.tensor_tensor(slot(wl, t), slot(raw, t), slot(wh, t).bitcast(F32), ALU.subtract).then_inc(lo_ready, 1)

            def lo_at(t):
                if t < TILES:
                    lo(t, t + 1)

            def strip_block(strip, n, last_tile):
                if n < NG - 1:
                    dve.wait_ge(banks_full, full_at(strip, n))
                else:
                    dve.wait_ge(tile_used, last_tile + 1)
                return bank[use_of(strip, n) % BANKS]

            def in_block(strip, n):
                return strip_block(strip, n, (strip + 1) * PER - 1)

            def x_part(q):
                for b in range(q * TK, (q + 1) * TK):
                    dve.wait_ge(x_hi, b + 1)
                    dve.scalar_tensor_tensor(out=XL[:, b, :], in0=X[:, b, :], scalar=v("norm_mix_g", b),
                                             in1=XH[:, b, :].bitcast(F32), op0=ALU.mult, op1=ALU.subtract).then_inc(x_lo, 1)

            def var_out(name, k_set=0):
                dve.wait_ge(misc_full, MISC_AT[name] + 1)
                dve.tensor_scalar(SETS[k_set][0], misc_bank(name)[:, 0:T], EPS, None, ALU.add).then_inc(var_ready, 1)

            def inv_root(k, dst, k_set=0, cols=slice(0, T), final=None):
                var, r, t = (x[:, cols] for x in SETS[k_set])
                dst = dst[:, cols]
                dve.wait_ge(sd_ready, k + 1)
                chain(dve.reciprocal(r, r))
                chain(dve.tensor_tensor(t, r, r, ALU.mult))
                chain(dve.scalar_tensor_tensor(out=t, in0=t, scalar=-0.5, in1=var, op0=ALU.mult, op1=ALU.mult))
                ins = dve.scalar_tensor_tensor(out=dst, in0=t, scalar=1.5, in1=r, op0=ALU.add, op1=ALU.mult)
                if final is not None:
                    ins.then_inc(final, 1)
                    dve.wait_ge(final, 1 + max(k - NORM["s3"], 0))
                else:
                    chain(ins)

            def fold(dst, src, i):
                dve.tensor_tensor(dst[:, 0:2, :], src[:, 0:2, :], src[:, 2:4, :], ALU.add).then_inc(halved, 1)
                dve.wait_ge(halved, i)
                dve.tensor_tensor(dst[:, 0, :], dst[:, 0, :], dst[:, 1, :], ALU.add).then_inc(quartered, 1)

            def scale_mixer(m, y, k, k_set=0):
                r = SETS[k_set][1]
                inv_root(k, r, k_set)
                for b in range(NG):
                    dve.scalar_tensor_tensor(out=y[:, b, :], in0=y[:, b, :], scalar=v("out_norm_g", m * NG + b),
                                             in1=r, op0=ALU.mult, op1=ALU.mult).then_inc(scaled[m], 1)

            def mixer_lo(m, y):
                for b in range(NG):
                    dve.wait_ge(mix_hi[m], b + 1)
                    dve.tensor_tensor(ML[:, m * NG + b, :], y[:, b, :], MH[:, m * NG + b, :].bitcast(F32),
                                      ALU.subtract).then_inc(mix_lo[m], 1)

            def conv_taps(n):
                for k in range(taps_done[0], taps_done[0] + n):
                    for b in range(VG):
                        src, acc = G[:, b, k:k + SEQ], T1[:, b, 0:SEQ]
                        if k == 0:
                            ins = dve.tensor_scalar(acc, src, tap(0, b), v("conv_a_b", b), ALU.mult, ALU.add)
                        else:
                            dve.wait_ge(conv_done, (k - 1) * VG + b + 1)
                            ins = dve.scalar_tensor_tensor(out=acc, in0=src, scalar=tap(k, b), in1=acc,
                                                           op0=ALU.mult, op1=ALU.add)
                        ins.then_inc(conv_done, 1)
                taps_done[0] += n

            def short_conv(b):
                for k in range(SW):
                    for h in range(2):
                        src, acc, w = c_at(b, k)[h], two(T2[:, b, :])[h], v("sconv_w", k * NG + b)
                        if k == 0:
                            ins = dve.tensor_scalar(acc, src, w, None, ALU.mult)
                        else:
                            ins = dve.scalar_tensor_tensor(out=acc, in0=src, scalar=w, in1=acc,
                                                           op0=ALU.mult, op1=ALU.add)
                        if h == 1:
                            chain(ins)
                chain(dve.tensor_tensor(T2[:, b, :], T2[:, b, :], s_bc[:, :], ALU.mult))

            def pooling(b):
                w = 2 << b
                src, width = PP[:, b, :], 1
                if b:
                    dve.wait_ge(pooled, b)
                for level in range(b + 1):
                    dst = (S_A, S_B)[level % 2]
                    start = 2 * width - 1
                    chain(dve.tensor_tensor(dst[:, start:PL], src[:, start:PL], src[:, start - width:PL - width], ALU.add))
                    src, width = dst, 2 * width
                assert width == w
                sums_at = (src[:, PW:PA], src[:, PA:PL].rearrange("p (s r) -> p s r", s=NB)[:, :, PW:PS])
                for h in range(2):
                    ins = dve.scalar_tensor_tensor(out=two(T2[:, b, :])[h], in0=sums_at[h], scalar=1.0 / w,
                                                   in1=p_at(b, PW)[h], op0=ALU.mult, op1=ALU.subtract)
                    chain(ins)
                head = sums_at[0][:, 0:w - 1]
                chain(dve.tensor_tensor(head, head, inv[:, 0:w - 1], ALU.mult))
                dve.tensor_tensor(T2[:, b, 0:w - 1], head, PP[:, b, PW:PW + w - 1], ALU.subtract).then_inc(pooled, 1)

            def residual(b, src):
                dve.tensor_tensor(X[:, b, :], src[:, 0:T], X[:, b, :], ALU.add).then_inc(banks_free, 1)

            def hidden(n, src):
                dve.tensor_tensor(HU[:, n, :], src[:, 0:T], SG[:, n, :], ALU.mult).then_inc(banks_free, 1)

            def hidden_lo(b, count):
                dve.wait_ge(h_hi, count)
                dve.tensor_tensor(ML[:, b, :], HU[:, b, :], MH[:, b, :].bitcast(F32), ALU.subtract).then_inc(h_lo, 1)

            def silu(count):
                for n in range(NG):
                    dve.wait_ge(ffn_sig, count + n + 1)
                    dve.tensor_tensor(SG[:, n, :], SG[:, n, :], T0[:, n, :], ALU.mult).then_inc(ffn_silu, 1)
                for n in range(NG):
                    dve.wait_ge(ffn_silu, count + n + 1)
                    dve.tensor_tensor(SG[:, n, :], SG[:, n, :], s_bc[:, :], ALU.mult).then_inc(ffn_scaled, 1)

            dve.wait_ge(vec_landed, 16)
            x_part(0)
            dve.wait_ge(first_hi, 1)
            dve.tensor_tensor(wl[:, 0:GRP], raw[:, 0:GRP], wh[:, 0:GRP].bitcast(F32), ALU.subtract).then_inc(first_lo, 1)
            dve.wait_ge(hi_ready, 1)
            dve.tensor_tensor(wl[:, GRP:TILE], raw[:, GRP:TILE], wh[:, GRP:TILE].bitcast(F32),
                              ALU.subtract).then_inc(lo_ready, 1)
            for q in range(1, AHEAD):
                x_part(q)
                lo_at(q)

            for t in range(T_LOOP):
                if t + AHEAD < XQ:
                    x_part(t + AHEAD)
                if t in VAR_AT:
                    var_out(VAR_AT[t], VAR_AT[t] in IN_PAIR)
                if t == 6:
                    inv_root(NORM["s1"], s_bc[:, :])
                if t == 7:
                    for n in range(NG):
                        src = in_block(0, n)
                        dve.tensor_tensor(T0[:, n, :], src[:, 0:T], s_bc[:, :], ALU.mult).then_inc(banks_free, 1)
                lo_at(t + AHEAD)
                if t in FOLDED:
                    W = (T1, T2, T4)[t]
                    dve.wait_ge(x_squares, t * NG + NG)
                    dve.tensor_tensor(W[:, 0:2, :], W[:, 0:2, :], W[:, 2:4, :], ALU.add).then_inc(x_folded, 1)
                if t in TAPS:
                    if t == 16:
                        dve.wait_ge(glu_ready, NG)
                        dve.wait_ge(pads_ready, 4)
                    conv_taps(TAPS[t])
                if t == 48:
                    dve.wait_ge(conv_p_done, (NG - VG) * CW - HANDED)
                    for i in range(HANDED):
                        k = CW - HANDED + i
                        if i:
                            dve.wait_ge(conv_done, CW * VG + i)
                        dve.scalar_tensor_tensor(out=T1[:, VG, 0:SEQ], in0=G[:, VG, k:k + SEQ], scalar=tap(k, VG),
                                                 in1=T1[:, VG, 0:SEQ], op0=ALU.mult, op1=ALU.add).then_inc(conv_done, 1)
                    dve.wait_ge(conv_done, CW * VG + HANDED)
                    dve.wait_ge(conv_s_done, NG - 1 + CW)
                    fold(B_SUM, T1, 4)
                if t == 8:
                    chain(dve.tensor_tensor(s2_bc[:, :], s_bc[:, :], s_bc[:, :], ALU.mult))
                if t == 9:
                    for n in range(NG):
                        dve.wait_ge(gate_sig, n + 1)
                        chain(dve.tensor_tensor(T0[:, n, :], T0[:, n, :], s_bc[:, :], ALU.mult))
                if t == 15:
                    dve.wait_ge(hist_landed, 48)
                    for n in range(NG):
                        src, dst, sig = two(in_block(1, n)[:, 0:T]), g_at(n, CW - 1), two(T0[:, n, :])
                        dve.tensor_tensor(dst[0], src[0], sig[0], ALU.mult).then_inc(glu_ready, 1)
                        dve.tensor_tensor(dst[1], src[1], sig[1], ALU.mult).then_inc(banks_free, 1)
                if t == 23:
                    for n in range(NG):
                        src, dst, s = two(in_block(2, n)[:, 0:T]), p_at(n, PW), two(s_bc[:, :])
                        dve.tensor_tensor(dst[0], src[0], s[0], ALU.mult).then_inc(pin_ready, 1)
                        dve.tensor_tensor(dst[1], src[1], s[1], ALU.mult).then_inc(banks_free, 1)
                if t == 24:
                    dve.wait_ge(banks_free, use_of(2, NG - 1) + 1)
                if 24 <= t <= 27:
                    pooling(t - 24)
                if t == 36:
                    dve.wait_ge(squares, 2 * NG)
                    fold(SQ, SQ, 3)
                if t == 41:
                    scale_mixer(MIX_B, T2, NORM["b_rms"], 1)
                if t == 48:
                    mixer_lo(MIX_B, T2)
                if t == 31:
                    for n in range(NG):
                        src = in_block(3, n)
                        dve.tensor_tensor(T0[:, n, :], src[:, 0:T], s_bc[:, :], ALU.mult).then_inc(banks_free, 1)
                if t == 32:
                    dve.wait_ge(squares, NG)
                    fold(SQ, SQ, 1)
                    dve.wait_ge(banks_free, use_of(3, NG - 1) + 1)
                    fold(B_SUM, T0, 2)
                if t == 34:
                    dve.wait_ge(misc_full, MISC_AT["d_mean"] + 1)
                    for n in range(NG):
                        dve.tensor_tensor(T0[:, n, :], T0[:, n, :], misc_bank("d_mean")[:, 0:T],
                                          ALU.subtract).then_inc(d_cent, 1)
                if t == 38:
                    inv_root(NORM["d_var"], SETS[0][1])
                if t == 39:
                    for n in range(NG):
                        src = in_block(4, n)
                        dve.tensor_tensor(T4[:, n, :], src[:, 0:T], s_bc[:, :], ALU.mult).then_inc(banks_free, 1)
                    for n in range(NG):
                        dve.tensor_tensor(T0[:, n, :], T0[:, n, :], SETS[0][1], ALU.mult).then_inc(d_unit, 1)
                if t in (45, 47):
                    for n in (0, 1) if t == 45 else (2, 3):
                        dve.wait_ge(banks_free, use_of(4, n) + 1)
                        dve.wait_ge(misc_full, MISC_AT[f"z{n}"] + 1)
                        dve.tensor_tensor(T4[:, n, :], misc_bank(f"z{n}")[:, 0:T], T4[:, n, :],
                                          ALU.mult).then_inc(d_out, 1)
                if t == DR + 1:
                    inv_root(NORM["d_rms"], SETS[0][1], final=d_rms_ready)
                if t == 47:
                    dve.wait_ge(misc_full, MISC_AT["vt2"] + 1)
                    dve.wait_ge(v_stored, 16)
                    for n in range(NG):
                        src = in_block(5, n)
                        dve.tensor_tensor(T0[:, n, :], src[:, 0:T], s2_bc[:, :], ALU.mult).then_inc(banks_free, 1)
                if t == 55:
                    for n in range(NG):
                        src, dst, ch = two(in_block(6, n)[:, 0:T]), c_at(n, SW - 1), two(T0[:, n, :])
                        dve.tensor_tensor(dst[0], src[0], ch[0], ALU.mult).then_inc(cin_ready, 1)
                        dve.tensor_tensor(dst[1], src[1], ch[1], ALU.mult).then_inc(banks_free, 1)
                if t == AM + 1:
                    dve.wait_ge(misc_full, MISC_AT["a_mean"] + 1)
                    for n in range(NG):
                        dve.tensor_tensor(T1[:, n, :], T1[:, n, :], misc_bank("a_mean")[:, 0:T],
                                          ALU.subtract).then_inc(a_cent, 1)
                if t in (57, 59):
                    dve.wait_ge(banks_free, use_of(6, NG - 1) + 1)
                    short_conv((57, 59).index(t))
                if t == AM + 4:
                    r = SETS[1][1]
                    inv_root(NORM["a_var"], r, 1)
                    for n in range(NG):
                        dve.tensor_tensor(T1[:, n, :], T1[:, n, :], r, ALU.mult).then_inc(a_unit, 1)
                if t == AM + 7:
                    for n in range(NG):
                        dve.wait_ge(a_act, n + 1)
                        dve.tensor_tensor(T1[:, n, :], T1[:, n, :], SG[:, n, :], ALU.mult).then_inc(a_out, 1)
                if t == AM + 11:
                    inv_root(NORM["a_rms"], SETS[1][1], 1, final=a_rms_ready)
                if t == 63:
                    dve.wait_ge(short_done, CG)
                    for n in range(NG):
                        src = in_block(7, n)
                        dve.tensor_tensor(T2[:, n, :], src[:, 0:T], T2[:, n, :], ALU.mult).then_inc(banks_free, 1)
                if t == 66:
                    mixer_lo(MIX_A, T1)
                if t == 66:
                    scale_mixer(MIX_C, T2, NORM["c_rms"])
                if t == 67:
                    mixer_lo(MIX_C, T2)
                if T_OUT <= t < T_G0 and t % PER == PER - 1:
                    for n in range(NG):
                        s = (t - T_OUT) // PER
                        residual(s * NG + n, strip_block(S_OUT + s, n, t))
                if T_OUT < t <= T_G0 and t % PER == 0:
                    for b in range((t - T_OUT) // PER * NG - NG, (t - T_OUT) // PER * NG):
                        dve.wait_ge(y_hi, b + 1)
                        dve.scalar_tensor_tensor(out=XL[:, b, :], in0=X[:, b, :], scalar=v("norm_ffn_g", b),
                                                 in1=XH[:, b, :].bitcast(F32), op0=ALU.mult,
                                                 op1=ALU.subtract).then_inc(y_lo, 1)
                if t == T_G0 + 4:
                    inv_root(NORM["s2"], s_bc[:, :])
                if t == T_U0 - 1:
                    for n in range(NG):
                        src = strip_block(S_G0, n, t)
                        dve.tensor_tensor(SG[:, n, :], src[:, 0:T], s_bc[:, :], ALU.mult).then_inc(banks_free, 1)
                if t == T_U0 + 1:
                    silu(0)
                if t == T_LOOP - 1:
                    dve.wait_ge(ffn_scaled, NG)
                    for n in range(NG):
                        hidden(n, strip_block(S_U0, n, t))
                        if n % TK == TK - 1:
                            for m in range(n - TK + 1, n + 1):
                                hidden_lo(m, m + 1)

            with dve.Fori(0, NF - 1) as g:
                def loop_block(i, n, j):
                    if n < NG - 1:
                        dve.wait_ge(banks_full, g * ((NG - 1) * S_BODY) + full_at(S_LOOP + i, n))
                    else:
                        dve.wait_ge(tile_used, g * BODY + (T_LOOP + j + 1))
                    return bank[use_of(S_LOOP + i, n) % BANKS]

                for j in range(BODY):
                    t = T_LOOP + j + AHEAD
                    if j < BODY - 1:
                        lo(t, g * BODY + (t + 1))
                    if j == PER - 1:
                        for n in range(NG):
                            src = loop_block(0, n, j)
                            dve.tensor_tensor(SG[:, n, :], src[:, 0:T], s_bc[:, :], ALU.mult).then_inc(banks_free, 1)
                    if PER < j < BODY - PER and j % PER_DN == PER_DN - 1:
                        s = (j - PER) // PER_DN
                        for n in range(NG):
                            residual(s * NG + n, loop_block(1 + s, n, j))
                    if j == PER + 2:
                        silu(g * NG + NG)
                    if j == BODY - 1:
                        dve.wait_ge(ffn_scaled, g * NG + 2 * NG)
                        for n in range(NG):
                            hidden(n, loop_block(S_BODY - 1, n, j))
                            if n % TK == TK - 1:
                                for m in range(n - TK + 1, n + 1):
                                    hidden_lo(m, g * NG + (NG + m + 1))
                        lo(t, g * BODY + (t + 1))
            for t in range(T_END, TILES):
                lo_at(t + AHEAD)
                if (t - T_END) % PER_DN == PER_DN - 1:
                    s = (t - T_END) // PER_DN
                    for n in range(NG):
                        residual(s * NG + n, strip_block(S_END + s, n, t))
            dve.wait_ge(last_sq, KD - NG + 2)
            dve.tensor_tensor(one_sq[:, :], SQ[:, 0, :], SQ[:, 1, :], ALU.add).then_inc(sums_dve, 1)

            dve.wait_ge(misc_full, MISC_AT["s3"] + 1)
            for h in PARTS:
                dve.tensor_scalar(SETS[0][0][:, h], misc_bank("s3")[:, h], EPS, None, ALU.add).then_inc(var_ready, 1)
            for i, h in enumerate(PARTS):
                inv_root(NORM["s3"] + i, s_bc[:, :], cols=h, final=s_final)
                s_all = s_bc[:, h].unsqueeze(1).to_broadcast([P, NG, h.stop - h.start])
                for m in range(YP[i] // NG, KD // NG):
                    bs = slice(m * NG, (m + 1) * NG)
                    dve.wait_ge(y_gained, (m + 1) * NG)
                    dve.tensor_tensor(X[:, bs, h], (T1, T2, T4, T0)[m][:, :, h], s_all, ALU.mult).then_inc(y_ready, 1)

        @block.tensor
        def _(pe):
            def into(name):
                i = MISC_AT[name]
                if i >= 2:
                    s, count = TAKEN[MISC[i - 2]]
                    pe.wait_ge(SEMS[s], count)
                return misc_bank(name)

            def mean_of(name, ready, src):
                M = into(name)
                pe.wait_ge(*ready)
                pe.matmul(M[:, 0:T], ones_g[:, :], src, start=True, stop=True).then_inc(misc_full, 1)

            def turn(name, parts):
                for out, in_ in parts:
                    k = in_.shape[0]
                    last = pe.transpose(out, in_, ident[0:k, 0:k])
                last.then_inc(misc_full, 1)

            def products(t, banks, moving, first, last, free_count, moving_ready=None):
                W_H, W_L = (slot(x, t).rearrange("p (k n) -> p k n", k=TK) for x in (wh, wl))
                if moving_ready is not None:
                    pe.wait_ge(*moving_ready)
                for n in range(NG):
                    if first and not (isinstance(free_count, int) and free_count + n <= 0):
                        pe.wait_ge(banks_free, free_count + n)
                    for k in range(TK):
                        hi_, lo_ = moving(k)
                        cols = slice(n * P, (n + 1) * P)
                        pe.matmul(banks[n][:, 0:T], W_H[:, k, cols], hi_, start=(first and k == 0), stop=False)
                        pe.matmul(banks[n][:, 0:T], W_H[:, k, cols], lo_, start=False, stop=False)
                        mm = pe.matmul(banks[n][:, 0:T], W_L[:, k, cols], hi_, start=False, stop=(last and k == TK - 1))
                    if last and n < NG - 1:
                        mm.then_inc(banks_full, 1)
                mm.then_inc(tile_used, 1)

            def strip_banks(strip):
                return [bank[use_of(strip, n) % BANKS] for n in range(NG)]

            def tile(t, strip, kt, tiles, xh, xl, base, moving_ready=None):
                pe.wait_ge(lo_ready, t + 1)
                products(t, strip_banks(strip), lambda k: (xh[:, base + k, :], xl[:, base + k, :]), kt == 0,
                         kt == tiles - 1, use_of(strip, 0) - BANKS + 1, moving_ready)

            pe.wait_ge(const_ready, 4)
            for _ in range(WARM):
                pe.matmul(bank[BANKS + 1][:, 0:P], ones[:, :], ones_d[:, :], start=True, stop=True)

            for k in range(TK):
                pe.wait_ge(*((first_lo, 1) if k == 0 else (lo_ready, 1)))
                pe.wait_ge(x_lo, k + 1)
                for n in range(NG):
                    w_h, w_l = (x[:, k * GRP + n * P:k * GRP + (n + 1) * P] for x in (wh, wl))
                    out = bank[n][:, 0:T]
                    pe.matmul(out, w_h, XH[:, k, :], start=(k == 0), stop=False)
                    pe.matmul(out, w_h, XL[:, k, :], start=False, stop=False)
                    mm = pe.matmul(out, w_l, XH[:, k, :], start=False, stop=False)
            mm.then_inc(tile_used, 1)

            for t in range(1, T_LOOP):
                if t < T_OUT:
                    s, kt = divmod(t, PER)
                    tile(t, s, kt, PER, XH, XL, kt * TK, (x_lo, kt * TK + TK) if s == 0 else None)
                elif t < T_G0:
                    s, kt = divmod(t - T_OUT, PER)
                    m, half = OUT_ORDER[kt // 2], kt % 2
                    tile(t, S_OUT + s, kt, PER, MH, ML, m * NG + half * TK,
                         (mix_lo[m], half * TK + TK) if s == 0 else None)
                else:
                    s, kt = divmod(t - T_G0, PER)
                    tile(t, S_G0 + s, kt, PER, XH, XL, kt * TK, (y_lo, kt * TK + TK) if s == 0 else None)
                if t == 5:
                    M = into("s1")
                    pe.wait_ge(const_ready, 4)
                    pe.wait_ge(sums, 1)
                    pe.matmul(M[:, 0:T], ones_d[:, :], sum_sq[:, :], start=True, stop=False)
                    pe.wait_ge(x_squares, KD)
                    pe.matmul(M[:, 0:T], ones_d[:, :], square_of(KD - 2), start=False, stop=False)
                    pe.matmul(M[:, 0:T], ones_d[:, :], square_of(KD - 1), start=False, stop=True).then_inc(misc_full, 1)
                if 28 <= t <= 29:
                    for b in (0, 1) if t == 28 else (2, 3):
                        M = into(f"b{b}")
                        pe.wait_ge(pooled, b + 1)
                        if b == 0:
                            pe.wait_ge(mats_landed, 32)
                        pe.matmul(M[:, 0:T], PWV[:, b, :], T2[:, b, :], start=True, stop=True).then_inc(misc_full, 1)
                if t == 33:
                    mean_of("b_rms", (quartered, 1), SQ[:, 0, :])
                    mean_of("d_mean", (quartered, 2), B_SUM[:, 0, :])
                if t == 37:
                    mean_of("d_var", (quartered, 3), SQ[:, 0, :])
                if 41 <= t <= 42:
                    pe.wait_ge(vn_ready, NG)
                    for c in (0, 1) if t == 41 else (2,):
                        M, n = into(f"vt{c}"), P if c < 2 else NB * NS
                        turn(f"vt{c}", [(M[0:n, b * P:(b + 1) * P], T0[:, b, c * P:c * P + n]) for b in range(NG)])
                if t in (44, 46):
                    pe.wait_ge(vt_ready, 3)
                    pe.wait_ge(masked, 1)
                    pe.wait_ge(corner_landed, 16 * NB)
                    for b in (0, 1) if t == 44 else (2, 3):
                        M, cols = into(f"z{b}"), slice(b * P, (b + 1) * P)
                        for c in range(2):
                            out = M[:, c * P:(c + 1) * P]
                            pe.matmul(out, vt[:, c, cols], WT[:, b, :], start=True, stop=False)
                            pe.matmul(out, ones[0:1, :], BROW[:, b, :], start=False, stop=True)
                        out = M[:, SEQ:T]
                        pe.matmul(out, vt[0:NB * NS, 2, cols], BD[:, b, :], start=True, stop=False)
                        bias = BROW[:, b, 0:NS].unsqueeze(1).to_broadcast([1, NB, NS])
                        pe.matmul(out, ones[0:1, :], bias, start=False, stop=True).then_inc(misc_full, 1)
                if t == AM:
                    mean_of("a_mean", (quartered, 4), B_SUM[:, 0, :])
                if t == DR:
                    mean_of("d_rms", (block_sum, 1), one_sq[:, :])
                if t == AM + 3:
                    mean_of("a_var", (block_sum, 2), one_sq[:, :])
                if t == AM + 10:
                    mean_of("a_rms", (block_sum, 3), one_sq[:, :])
                if t == 65:
                    mean_of("c_rms", (block_sum, 4), one_sq[:, :])
                if t == T_G0 + 3:
                    M = into("s2")
                    pe.wait_ge(sums, 2)
                    pe.matmul(M[:, 0:T], ones_d[:, :], sum_sq[:, :], start=True, stop=True).then_inc(misc_full, 1)

            with pe.Fori(0, NF - 1) as g:
                for j in range(BODY):
                    t = T_LOOP + j
                    down = PER <= j < BODY - PER
                    if down:
                        i, kt = (j - PER) // PER_DN + 1, (j - PER) % PER_DN
                        tiles, xh, xl, base = PER_DN, MH, ML, kt * TK
                    else:
                        i, kt = (0, j) if j < PER else (S_BODY - 1, j - (BODY - PER))
                        tiles, xh, xl, base = PER, XH, XL, kt * TK
                    pe.wait_ge(lo_ready, g * BODY + (t + 1))
                    products(t, strip_banks(S_LOOP + i), lambda k: (xh[:, base + k, :], xl[:, base + k, :]), kt == 0,
                             kt == tiles - 1, g * (NG * S_BODY) + (use_of(S_LOOP + i, 0) - BANKS + 1),
                             (h_lo, g * NG + NG) if j == PER else None)
            for t in range(T_END, TILES):
                s, kt = divmod(t - T_END, PER_DN)
                tile(t, S_END + s, kt, PER_DN, MH, ML, kt * TK, (h_lo, (NF - 1) * NG + kt * TK + TK) if s == 0 else None)

            M = into("s3")
            pe.wait_ge(sums, 3)
            pe.matmul(M[:, 0:T], ones_d[:, :], sum_sq[:, :], start=True, stop=False)
            pe.wait_ge(last_sq, KD - 1)
            pe.matmul(M[:, 0:T], ones_d[:, :], SQ[:, NG - 2, :], start=False, stop=False)
            pe.wait_ge(sums_dve, 1)
            pe.matmul(M[:, 0:T], ones_d[:, :], one_sq[:, :], start=False, stop=False)
            pe.wait_ge(last_sq, KD)
            pe.matmul(M[:, 0:T], ones_d[:, :], SQ[:, NG - 1, :], start=False, stop=True).then_inc(misc_full, 1)


def kernel(**inputs):
    import numpy as np
    import concourse.bacc as bacc
    from concourse.bass_utils import run_bass_kernel_spmd

    def rows(name):
        return np.asarray(inputs[name]).reshape(-1, P).T

    def history(name, width, new):
        h = np.asarray(inputs[name])[0].reshape(NB, width, NG, P).transpose(3, 2, 0, 1)
        return np.pad(h, ((0, 0), (0, 0), (0, 0), (0, new))).reshape(P, NG, NB * (width + new))

    tokens = np.concatenate([np.asarray(inputs["x_prompt"])[0], np.asarray(inputs["x_sample"]).reshape(NB * NS, D)])
    host = {
        "x": tokens.reshape(T, KD, P).transpose(2, 1, 0),
        "vec": np.concatenate([rows(name) for name, _ in VECS], axis=1),
        "hist_a": history("state_conv_a", CW - 1, NS),
        "hist_p": history("state_pool", PW, NS),
        "hist_c": history("state_sconv", SW - 1, NS),
        "sgu_wt": np.asarray(inputs["sgu_w"])[0].transpose(2, 0, 1),
    }
    for name in ("w_in", "w_out", "w_gate", "w_up", "w_down", "pool_w", "sgu_b"):
        host[name] = np.asarray(inputs[name])[0]
    shapes = {"y": (P, KD, T), "a": (P, NG, GL - SEQ), "p": (P, NG, PL - SEQ), "c": (P, NG, CL - SEQ),
              "v": (P, NG, NB * NS)}

    nc = bacc.Bacc("TRN2", target_bir_lowering=False, num_devices=1)
    arrays, ins = {}, {}
    for name, x in host.items():
        x = np.ascontiguousarray(x)
        arrays[f"in_{name}"] = x
        ins[name] = nc.dram_tensor(f"in_{name}", x.shape, mybir.dt.from_np(x.dtype), kind="ExternalInput").ap()
    outs = {n: nc.dram_tensor(f"out_{n}", s, F32, kind="ExternalOutput").ap() for n, s in shapes.items()}
    hybrid_step(nc, ins, outs)
    got = run_bass_kernel_spmd(nc, [arrays], core_ids=[0]).results[0]

    y = got["out_y"].transpose(2, 1, 0).reshape(T, D)

    def state(x, kept):
        def last(r):
            r = r[..., -kept:]
            return np.ascontiguousarray(r.transpose(2, 3, 1, 0).reshape(1, -1, kept, GRP))
        return last(x[:, :, None, :kept]), last(x[:, :, kept:].reshape(P, NG, NB, -1))

    new_a, new_p, new_c = (state(got[f"out_{n}"], k) for n, k in (("a", CW - 1), ("p", PW), ("c", SW - 1)))
    chunk_v = got["out_v"].transpose(2, 1, 0).reshape(1, NB, NS, GRP)
    return (np.ascontiguousarray(y[:SEQ]).reshape(1, SEQ, D), np.ascontiguousarray(y[SEQ:]).reshape(NB, NS, D),
            *new_a, *new_p, *new_c, np.ascontiguousarray(chunk_v))
```
